# Optimizing a Trainium2 kernel written in Bass

```python
import jax, jax.numpy as jnp
from jax import lax
import numpy as np

D_MODEL = 1024
BATCH = 1
SEQ = 512
DEPTH = 1

D_MIX = D_MODEL
N_HEADS_A = 8
HEAD_DIM_A = 64
D_A = N_HEADS_A * HEAD_DIM_A
N_IDX_HEADS = 8
IDX_DIM = 32
TOPK_MAX = 256
Q_BLOCK = 128
N_HEADS_M = 4
HEAD_DIM_M = 128
D_M = N_HEADS_M * HEAD_DIM_M
CONV_K = 4
CHUNK = 64
N_GROUPS = 4
EXPERTS_PER_GROUP = 8
N_EXPERTS = N_GROUPS * EXPERTS_PER_GROUP
TOP_K_EXPERTS = 2
D_EXPERT = 256
D_PLE = 256
LN_EPS = 1e-5
NEG_BIG = -1e30
DEEPNORM_ALPHA = (2.0 * DEPTH) ** 0.25
DEEPNORM_BETA = (8.0 * DEPTH) ** -0.25
IN_SPLITS = (D_A, D_A, D_A, N_IDX_HEADS * IDX_DIM, IDX_DIM, N_IDX_HEADS, D_M, D_M, D_M, D_M, N_HEADS_M, N_HEADS_M)
D_IN_PROJ = 3 * D_A + N_IDX_HEADS * IDX_DIM + IDX_DIM + N_IDX_HEADS + 4 * D_M + 2 * N_HEADS_M

kernel_name = 'hymba_dsa_mlstm_hiermoe_deepnorm'

def _layer_norm(x, g, b):
    xf = x.astype(jnp.float32)
    mu = jnp.mean(xf, axis=-1, keepdims=True)
    var = jnp.mean(jnp.square(xf - mu), axis=-1, keepdims=True)
    y = (xf - mu) * lax.rsqrt(var + LN_EPS)
    return (y * g.astype(jnp.float32) + b.astype(jnp.float32)).astype(x.dtype)

def _causal_depthwise_conv(x, w, b):
    S = x.shape[1]
    xp = jnp.pad(x, ((0, 0), (CONV_K - 1, 0), (0, 0)))
    out = b
    for j in range(CONV_K):
        out = out + w[j] * xp[:, j:j + S]
    return out

def _dsa_attention(q, k, v, q_idx, k_idx, w_idx):
    B, S = q.shape[0], q.shape[1]
    topk = min(TOPK_MAX, S // 4)
    n_blocks = S // Q_BLOCK
    slopes = jnp.exp2(-8.0 * jnp.arange(1, N_HEADS_A + 1, dtype=jnp.float32) / N_HEADS_A)
    k_idx_f = k_idx.astype(jnp.float32)
    key_pos = jnp.arange(S, dtype=jnp.int32)

    def to_blocks(a):
        return jnp.swapaxes(a.reshape((B, n_blocks, Q_BLOCK) + a.shape[2:]), 0, 1)

    def attend_block(args):
        qb, qib, wb, blk = args
        t = blk * Q_BLOCK + jnp.arange(Q_BLOCK, dtype=jnp.int32)
        logits = jnp.einsum('bqhd,bsd->bqhs', qib.astype(jnp.float32), k_idx_f) * IDX_DIM ** -0.5
        w_heads = wb.astype(jnp.float32) * N_IDX_HEADS ** -0.5
        score = jnp.einsum('bqh,bqhs->bqs', w_heads, jax.nn.relu(logits))
        score = jnp.where(key_pos[None, None, :] <= t[None, :, None], score, NEG_BIG)
        _, idx = lax.top_k(score, topk)
        k_sel = jax.vmap(lambda kb, ib: kb[ib])(k, idx)
        v_sel = jax.vmap(lambda vb, ib: vb[ib])(v, idx)
        s = jnp.einsum('bqhd,bqkhd->bhqk', qb, k_sel).astype(jnp.float32) * HEAD_DIM_A ** -0.5
        dist = (t[None, :, None] - idx).astype(jnp.float32)
        s = s - slopes[None, :, None, None] * dist[:, None]
        s = jnp.where((idx <= t[None, :, None])[:, None], s, -jnp.inf)
        prob = jax.nn.softmax(s, axis=-1).astype(v.dtype)
        return jnp.einsum('bhqk,bqkhd->bqhd', prob, v_sel)

    out = lax.map(attend_block, (to_blocks(q), to_blocks(q_idx), to_blocks(w_idx),
                                 jnp.arange(n_blocks, dtype=jnp.int32)))
    return jnp.swapaxes(out, 0, 1).reshape(B, S, D_A)

def _mlstm(q, k, v, i_pre, f_pre, o_pre, gn_w):
    B, S = q.shape[0], q.shape[1]
    nc = S // CHUNK
    f32 = jnp.float32

    def chunks(a):
        return a.astype(f32).reshape(B, nc, CHUNK, N_HEADS_M, HEAD_DIM_M).transpose(1, 0, 3, 2, 4)

    def gate_chunks(a):
        return a.reshape(B, nc, CHUNK, N_HEADS_M).transpose(1, 0, 3, 2)

    qc = chunks(q) * HEAD_DIM_M ** -0.5
    kc, vc = chunks(k), chunks(v)
    ic = gate_chunks(i_pre.astype(f32))
    fc = gate_chunks(jax.nn.log_sigmoid(f_pre.astype(f32)))
    causal = jnp.tril(jnp.ones((CHUNK, CHUNK), dtype=bool))

    def step(carry, inp):
        C, n, m = carry
        qb, kb, vb, ib, fb = inp
        b_cum = jnp.cumsum(fb, axis=-1)
        d_log = jnp.where(causal, b_cum[..., :, None] - b_cum[..., None, :] + ib[..., None, :], -jnp.inf)
        inter = b_cum + m[..., None]
        m_t = jnp.maximum(inter, jnp.max(d_log, axis=-1))
        w_intra = jnp.einsum('bhtd,bhsd->bhts', qb, kb) * jnp.exp(d_log - m_t[..., None])
        w_inter = jnp.exp(inter - m_t)
        num = jnp.einsum('bhts,bhsv->bhtv', w_intra, vb) + w_inter[..., None] * jnp.einsum('bhtd,bhdv->bhtv', qb, C)
        den = jnp.sum(w_intra, axis=-1) + w_inter * jnp.einsum('bhtd,bhd->bht', qb, n)
        h = num / jnp.maximum(jnp.abs(den), jnp.exp(-m_t))[..., None]
        b_last = b_cum[..., -1]
        w_log = b_last[..., None] - b_cum + ib
        m_new = jnp.maximum(b_last + m, jnp.max(w_log, axis=-1))
        decay = jnp.exp(b_last + m - m_new)
        w_in = jnp.exp(w_log - m_new[..., None])
        C_new = decay[..., None, None] * C + jnp.einsum('bhs,bhsd,bhsv->bhdv', w_in, kb, vb)
        n_new = decay[..., None] * n + jnp.einsum('bhs,bhsd->bhd', w_in, kb)
        return (C_new, n_new, m_new), h

    init = (jnp.zeros((B, N_HEADS_M, HEAD_DIM_M, HEAD_DIM_M), f32),
            jnp.zeros((B, N_HEADS_M, HEAD_DIM_M), f32),
            jnp.zeros((B, N_HEADS_M), f32))
    _, hc = lax.scan(step, init, (qc, kc, vc, ic, fc))
    h = hc.transpose(1, 0, 3, 2, 4).reshape(B, S, N_HEADS_M, HEAD_DIM_M)
    mu = jnp.mean(h, axis=-1, keepdims=True)
    var = jnp.mean(jnp.square(h - mu), axis=-1, keepdims=True)
    h = ((h - mu) * lax.rsqrt(var + LN_EPS)).reshape(B, S, D_M) * gn_w.astype(f32)
    return (jax.nn.sigmoid(o_pre.astype(f32)) * h).astype(q.dtype)

def _hierarchical_moe(x, rg_w, rg_b, re_w, re_b, e_gate, e_up, e_down):
    B, S, D = x.shape
    xt = x.reshape(B * S, D)
    g_prob = jax.nn.softmax((xt @ rg_w + rg_b).astype(jnp.float32), axis=-1)
    g_sel = jnp.argmax(g_prob, axis=-1)
    g_p = jnp.take_along_axis(g_prob, g_sel[:, None], axis=-1)[:, 0]
    e_logit = (xt @ re_w + re_b).astype(jnp.float32).reshape(-1, N_GROUPS, EXPERTS_PER_GROUP)
    e_logit = jnp.take_along_axis(e_logit, g_sel[:, None, None], axis=1)[:, 0]
    e_prob = jax.nn.softmax(e_logit, axis=-1)
    top_w, top_i = lax.top_k(e_prob, TOP_K_EXPERTS)
    top_w = top_w / jnp.sum(top_w, axis=-1, keepdims=True)
    w_local = jnp.einsum('nk,nke->ne', top_w, jax.nn.one_hot(top_i, EXPERTS_PER_GROUP, dtype=jnp.float32))
    comb = (jax.nn.one_hot(g_sel, N_GROUPS, dtype=jnp.float32)[:, :, None]
            * w_local[:, None, :] * g_p[:, None, None]).astype(x.dtype)
    y = jnp.zeros_like(xt)
    for g in range(N_GROUPS):
        sl = slice(g * EXPERTS_PER_GROUP, (g + 1) * EXPERTS_PER_GROUP)
        h = jax.nn.silu(jnp.einsum('nd,edf->nef', xt, e_gate[sl])) * jnp.einsum('nd,edf->nef', xt, e_up[sl])
        h = h * comb[:, g, :, None]
        y = y + jnp.einsum('nef,efd->nd', h, e_down[sl])
    return y.reshape(B, S, D)

def _hybrid_layer(x, p_i, w_in, b_igate, b_fgate, conv_w, conv_b, gn_w, w_out, ln1_g, ln1_b,
                  rg_w, rg_b, re_w, re_b, e_gate, e_up, e_down, ln2_g, ln2_b, ple_gate_w, ple_proj_w):
    B, S, _ = x.shape
    z = x @ w_in
    split_points = [int(c) for c in np.cumsum(IN_SPLITS)[:-1]]
    q_a, k_a, v_a, q_idx, k_idx, w_idx, q_m, k_m, v_m, o_m, i_m, f_m = jnp.split(z, split_points, axis=-1)
    shape_a = (B, S, N_HEADS_A, HEAD_DIM_A)
    y_a = _dsa_attention(q_a.reshape(shape_a), k_a.reshape(shape_a), v_a.reshape(shape_a),
                         q_idx.reshape(B, S, N_IDX_HEADS, IDX_DIM), k_idx, w_idx)
    qk_m = jax.nn.silu(_causal_depthwise_conv(jnp.concatenate([q_m, k_m], axis=-1), conv_w, conv_b))
    q_m, k_m = jnp.split(qk_m, 2, axis=-1)
    shape_m = (B, S, N_HEADS_M, HEAD_DIM_M)
    y_m = _mlstm(q_m.reshape(shape_m), k_m.reshape(shape_m), v_m.reshape(shape_m),
                 i_m + b_igate, f_m + b_fgate, o_m, gn_w)
    mix = jnp.concatenate([y_a, y_m], axis=-1) @ w_out
    x = _layer_norm(DEEPNORM_ALPHA * x + mix, ln1_g, ln1_b)
    ffn = _hierarchical_moe(x, rg_w, rg_b, re_w, re_b, e_gate, e_up, e_down)
    x = _layer_norm(DEEPNORM_ALPHA * x + ffn, ln2_g, ln2_b)
    return x + jax.nn.sigmoid(x @ ple_gate_w) * (p_i @ ple_proj_w)

def setup_inputs(seed: int = 0) -> dict:
    key = jax.random.key(seed)
    ks = jax.random.split(key, 24)

    def nrm(k, shape, scale):
        return scale * jax.random.normal(k, shape, jnp.float32)

    col_scale = jnp.concatenate([jnp.full((n,), DEEPNORM_BETA if j in (2, 8) else 1.0, jnp.float32)
                                 for j, n in enumerate(IN_SPLITS)])
    return {
        'x': nrm(ks[0], (BATCH, SEQ, D_MODEL), 1.0),
        'p': nrm(ks[1], (DEPTH, BATCH, SEQ, D_PLE), 1.0),
        'w_in': nrm(ks[2], (DEPTH, D_MODEL, D_IN_PROJ), D_MODEL ** -0.5) * col_scale,
        'b_igate': nrm(ks[3], (DEPTH, N_HEADS_M), 0.1),
        'b_fgate': jnp.linspace(3.0, 6.0, N_HEADS_M, dtype=jnp.float32)[None] + nrm(ks[4], (DEPTH, N_HEADS_M), 0.01),
        'conv_w': nrm(ks[5], (DEPTH, CONV_K, 2 * D_M), CONV_K ** -0.5),
        'conv_b': nrm(ks[6], (DEPTH, 2 * D_M), 0.01),
        'gn_w': 1.0 + nrm(ks[7], (DEPTH, D_M), 0.01),
        'w_out': nrm(ks[8], (DEPTH, D_MIX, D_MODEL), D_MIX ** -0.5 * DEEPNORM_BETA),
        'ln1_g': 1.0 + nrm(ks[9], (DEPTH, D_MODEL), 0.01),
        'ln1_b': nrm(ks[10], (DEPTH, D_MODEL), 0.01),
        'router_group_w': nrm(ks[11], (DEPTH, D_MODEL, N_GROUPS), D_MODEL ** -0.5),
        'router_group_b': nrm(ks[12], (DEPTH, N_GROUPS), 0.01),
        'router_expert_w': nrm(ks[13], (DEPTH, D_MODEL, N_EXPERTS), D_MODEL ** -0.5),
        'router_expert_b': nrm(ks[14], (DEPTH, N_EXPERTS), 0.01),
        'expert_w_gate': nrm(ks[15], (DEPTH, N_EXPERTS, D_MODEL, D_EXPERT), D_MODEL ** -0.5),
        'expert_w_up': nrm(ks[16], (DEPTH, N_EXPERTS, D_MODEL, D_EXPERT), D_MODEL ** -0.5),
        'expert_w_down': nrm(ks[17], (DEPTH, N_EXPERTS, D_EXPERT, D_MODEL), D_EXPERT ** -0.5 * DEEPNORM_BETA),
        'ln2_g': 1.0 + nrm(ks[18], (DEPTH, D_MODEL), 0.01),
        'ln2_b': nrm(ks[19], (DEPTH, D_MODEL), 0.01),
        'ple_gate_w': nrm(ks[20], (DEPTH, D_MODEL, D_MODEL), D_MODEL ** -0.5),
        'ple_proj_w': nrm(ks[21], (DEPTH, D_PLE, D_MODEL), D_PLE ** -0.5),
    }

def reference(x, p, w_in, b_igate, b_fgate, conv_w, conv_b, gn_w, w_out, ln1_g, ln1_b,
              router_group_w, router_group_b, router_expert_w, router_expert_b,
              expert_w_gate, expert_w_up, expert_w_down, ln2_g, ln2_b, ple_gate_w, ple_proj_w):
    for i in range(DEPTH):
        x = _hybrid_layer(x, p[i], w_in[i], b_igate[i], b_fgate[i], conv_w[i], conv_b[i], gn_w[i],
                          w_out[i], ln1_g[i], ln1_b[i], router_group_w[i], router_group_b[i],
                          router_expert_w[i], router_expert_b[i], expert_w_gate[i], expert_w_up[i],
                          expert_w_down[i], ln2_g[i], ln2_b[i], ple_gate_w[i], ple_proj_w[i])
    return x


_drawn_inputs = setup_inputs


def setup_inputs(seed=0):
    import zlib

    import numpy as np

    out = dict(_drawn_inputs(seed))
    spreads = {}
    factors = {'b_igate': 64.0,
     'conv_b': 8.0,
     'gn_w': 8.0,
     'ln1_g': 4.233,
     'ln1_b': 3.397,
     'router_group_b': 6.17,
     'router_expert_b': 7.32,
     'ln2_g': 200.0,
     'ln2_b': 200.0,
     'p': 3.04,
     'ple_gate_w': 4.358,
     'ple_proj_w': 3.051}
    for name, (base, spread) in spreads.items():
        noise = np.random.default_rng([zlib.crc32(name.encode()), seed]).standard_normal(out[name].shape)
        drawn = base * np.exp(spread * noise) if base else spread * noise
        out[name] = __import__('jax').numpy.asarray(drawn.astype(out[name].dtype))
    for name, factor in factors.items():
        out[name] = (out[name] * factor).astype(out[name].dtype)
    return out
```

```python
import concourse.bass as bass
from concourse import mybir
from contextlib import ExitStack

F32 = mybir.dt.float32
F32R = mybir.dt.float32r
BF16 = mybir.dt.bfloat16
I32 = mybir.dt.int32
ALU = mybir.AluOpType
ACT = mybir.ActivationFunctionType
AXX = mybir.AxisListType.X

P = 128
SEQ, DM = 512, 1024
NT, NK = SEQ // P, DM // P
HA, DA = 8, 64
HI_, DI = 8, 32
HM = 4
TOPK = min(256, SEQ // 4)
ALPHA = 2.0 ** 0.25
EPS = 1e-5
NG = 4
PIECES = 7
SMALL = 3
NPIECE = SMALL + NG * PIECES
PW = NK * P
NE, EG, GROUPS = 32, 8, 4
DE = 256
BLOCKS = SEQ // P
GW = 2048
SKIP = 4096
BIG = 1.0e30
TAKEN = -3.0e38


def hybrid_layer(nc, d, out, x1_dram, pair_dram):
    ctx = ExitStack()
    with ctx:
        def sb(name, shape, dt=F32):
            return ctx.enter_context(nc.sbuf_tensor(name, shape, dt))

        def sem(name):
            return ctx.enter_context(nc.semaphore(name))

        raw = sb("raw", [P, 12 * PW])
        w_hi = sb("w_hi", [P, 6 * PW], F32R)
        w_lo = sb("w_lo", [P, 6 * PW], F32R)
        a_hi = sb("a_hi", [P, NK, SEQ], F32R)
        a_lo = sb("a_lo", [P, NK, SEQ], F32R)
        res = sb("res", [P, NT * DM])
        y = sb("y", [P, NT, DM])
        pa = sb("pa", [P, 9536])

        ident = sb("ident", [P, P])
        sel_head = sb("sel_head", [HM, HM, P])
        dist = sb("dist", [P, SEQ])
        q_scale = sb("q_scale", [P, NG])
        conv_wb = sb("conv_wb", [P, 2 * HM, 5])
        gn_half = sb("gn_half", [P, HM * P])
        if_bias = sb("if_bias", [P, 8])
        w16_hi = sb("w16_hi", [P, NK, 16], F32R)
        w16_lo = sb("w16_lo", [P, NK, 16], F32R)
        w_head = sb("w_head", [P, NT, HI_])
        if_pre = sb("if_pre", [P, NT, 8])
        a_col = sb("a_col", [P, NT, HM])
        em_col = sb("em_col", [P, NT, HM])
        small = sb("small", [P, 160])
        tri = sb("tri", [P, P], BF16)
        ones = sb("ones", [P, P], BF16)
        chosen = sb("chosen", [P, NT, NE], BF16)
        row_got, row_put = sb("row_got", [P, NE], I32), sb("row_put", [P, NE], I32)
        at_got, at_put = sb("at_got", [P, 2], I32), sb("at_put", [P, 2], I32)
        most = sb("most", [P, 1], I32)

        bank = [ctx.enter_context(nc.psum_tensor(f"bank{i}", [P, 512], F32)) for i in range(8)]
        proj_bank = bank[0:2]
        score_bank = bank[2:4]
        turn_bank, attn_bank = bank[4], bank[5]
        lstm_bank = bank[6:8]

        x_raw = res[:, :].rearrange("p (k t) -> p k t", k=NK)
        RAWS = 5
        scratch = raw[:, RAWS * PW:12 * PW]
        qi = scratch[:, 0:1024].rearrange("p (a t) -> p a t", a=2)
        ki = scratch[:, 1024:1536]
        relu = scratch[:, 1536:2560].rearrange("p (a s) -> p a s", a=2)
        SO = [None, 0, 256, 640]
        score = scratch[:, 2560:3712]
        left = scratch[:, 3712:4864]
        i_row = scratch[0:HM, 4864:5376]
        f_row = scratch[0:HM, 5376:5888]
        c_row = scratch[0:HM, 5888:6400]
        g_row = scratch[0:HM, 6400:6912]
        w16 = scratch[:, 6912:7040].rearrange("p (k c) -> p k c", k=NK)
        masked = scratch[:, 0:1024].rearrange("p (a s) -> p a s", a=2)
        prob = scratch[:, 1024:2048].rearrange("p (a s) -> p a s", a=2)
        prob_t = scratch[:, 2048:3072].rearrange("p (a s) -> p a s", a=2)
        LO_ = [0, 512, 896, 1152, 1280]
        decay = res[:, 0:1280]
        weight = res[:, 1280:2560]
        conv = res[:, 2560:3584].rearrange("p (a t) -> p a t", a=2)
        tanh_c = res[:, 3584:4096]

        at = [0]

        def take(n):
            at[0] += n
            return pa[:, at[0] - n:at[0]]

        q_t = take(1024).rearrange("p (a t) -> p a t", a=2)
        k_t = take(1024).rearrange("p (a t) -> p a t", a=2)
        v_a = take(1024).rearrange("p (a s c) -> p a s c", a=2, s=NT)
        mdist = take(1280)
        MO = [0, 128, 384, 768]
        pre = take(2 * 516).rearrange("p (a t) -> p a t", a=2)
        qk_m = take(1024).rearrange("p (a t) -> p a t", a=2)
        v_m = take(2 * NT * 129).rearrange("p (a s c) -> p a s c", a=2, s=NT)
        o_m = take(1024).rearrange("p (a s c) -> p a s c", a=2, s=NT)
        hidden = take(NT * 129).rearrange("p (s c) -> p s c", s=NT)
        nega_row = take(512)[0:HM, :]
        assert at[0] <= 9536, at

        row_max = small[:, 0:2]
        neg_max = small[:, 2:4]
        row_sum = small[:, 8:16].rearrange("p (t h) -> p t h", h=2)
        row_inv = small[:, 16:24].rearrange("p (t h) -> p t h", h=2)
        best = small[:, 24:48].rearrange("p (b n) -> p b n", b=3)
        den = small[:, 48:52]
        den_inv = small[:, 52:56]
        stats = small[:, 56:80].rearrange("p (s c) -> p s c", s=NT)
        mean_var = small[:, 80:88].rearrange("p (s c) -> p s c", s=NT)
        rstd = small[:, 88:92]
        minus_half = small[:, 92:96]

        ple = pa[:, 0:4096].rearrange("p (t c) -> p t c", t=NT)
        ln_g, ln_b = pa[:, 4096:5120], pa[:, 5120:6144]
        at[0] = 6144
        logit = take(NT * 36).rearrange("p (t c) -> p t c", t=NT)
        r_bias = take(36)
        one_g, eq_g, dif_g = [take(NT * GROUPS).rearrange("p (t g) -> p t g", t=NT) for _ in range(3)]
        one_e = [take(NT * EG).rearrange("p (t e) -> p t e", t=NT) for _ in range(2)]
        e_log, eq_e = [take(NT * EG).rearrange("p (t e) -> p t e", t=NT) for _ in range(2)]
        picked = take(NT * NE).rearrange("p (t e g) -> p t e g", t=NT, e=EG)
        col = [take(NT) for _ in range(16)]
        one = [take(NT * NE).rearrange("p (t e) -> p t e", t=NT) for _ in range(2)]
        tok = [take(NT * NE).rearrange("p (t e) -> p t e", t=NT) for _ in range(2)]
        twice = take(NT * NE).rearrange("p (t e) -> p t e", t=NT)
        place = take(NT * NE).rearrange("p (t e) -> p t e", t=NT)
        seat = [take(NT * P).rearrange("p (t c) -> p t c", t=NT) for _ in range(2)]
        count_c = take(P)
        rank = take(EG)
        token = take(NT)
        skip_row = take(1)
        silu_g = take(DE)
        h_buf = take(DE)
        assert at[0] <= 9536, at
        y_flat = y[:, :, :].rearrange("p t c -> p (t c)")
        x_got = [y_flat[:, i * DM:(i + 1) * DM] for i in range(2)]
        y_out = [y_flat[:, (2 + i) * DM:(3 + i) * DM] for i in range(2)]
        hi_flat = a_hi[:, :, :].rearrange("p k t -> p (k t)")
        lo_flat = a_lo[:, :, :].rearrange("p k t -> p (k t)")

        def xg(m, par):
            return m[:, par * DM:(par + 1) * DM].rearrange("p (k c) -> p k c", k=NK)

        def ht(m):
            return m[:, 2 * DM:2 * DM + DE].rearrange("p (k c) -> p k c", k=2)

        wr_raw = raw[:, 7168:7168 + NK * 36].rearrange("p (k c) -> p k c", k=NK)
        stat8 = small[:, 0:48].rearrange("p (t c) -> p t c", t=NT)
        mv8 = small[:, 48:56].rearrange("p (t c) -> p t c", t=NT)
        rs8 = small[:, 56:60]
        ve8 = small[:, 60:64]
        gate_w = [small[:, 64:68], small[:, 68:72]]
        p_raw = raw[:, 6144:7168].rearrange("p (k t) -> p k t", k=2)
        WR_AT = 3 * GW - NK * 36

        s_x = [sem(f"s_x{c}") for c in range(4)]
        s_const = sem("s_const")
        s_w16 = sem("s_w16")
        s_raw = [sem(f"s_raw{i}") for i in range(RAWS)]
        s_xhi, s_xlo = sem("s_xhi"), sem("s_xlo")
        s_w16s = sem("s_w16s")
        s_whi, s_wlo = sem("s_whi"), sem("s_wlo")
        s_proj, s_evac = sem("s_proj"), sem("s_evac")
        s_setup = sem("s_setup")
        s_gate_p, s_gate_e = sem("s_gate_p"), sem("s_gate_e")
        s_row_p, s_row_v, s_row_a = sem("s_row_p"), sem("s_row_v"), sem("s_row_a")
        s_col_p, s_col_v = sem("s_col_p"), sem("s_col_v")
        s_idx, s_relu, s_acc = sem("s_idx"), sem("s_relu"), sem("s_acc")
        s_fut = sem("s_fut")
        s_top, s_mdist, s_md0 = sem("s_top"), sem("s_mdist"), sem("s_md0")
        s_qk, s_masked, s_negmax, s_exp = sem("s_qk"), sem("s_masked"), sem("s_negmax"), sem("s_exp")
        s_turn, s_probt, s_pv = sem("s_turn"), sem("s_probt"), sem("s_pv")
        s_yinv, s_ya = sem("s_yinv"), sem("s_ya")
        s_gbc, s_gadd, s_dexp, s_dmask = sem("s_gbc"), sem("s_gadd"), sem("s_dexp"), sem("s_dmask")
        s_mqk, s_mw, s_mnum, s_hid = sem("s_mqk"), sem("s_mw"), sem("s_mnum"), sem("s_hid")
        s_cacc, s_ctanh, s_conv = sem("s_cacc"), sem("s_ctanh"), sem("s_conv")
        s_post, s_var, s_pow, s_ym = sem("s_post"), sem("s_var"), sem("s_pow"), sem("s_ym")
        s_idle = sem("s_idle")
        s_or = [sem(f"s_or{q}") for q in range(4)]
        s_ohi, s_olo, s_wo = sem("s_ohi"), sem("s_olo"), sem("s_wo")
        s_yt, s_yhi, s_ylo = sem("s_yt"), sem("s_yhi"), sem("s_ylo")
        s_xn = [sem(f"s_xn{t}") for t in range(NT)]
        s_lnw, s_lnw2 = sem("s_lnw"), sem("s_lnw2")
        s_r, s_bn, s_ve, s_rs, s_ln = sem("s_r"), sem("s_bn"), sem("s_ve"), sem("s_rs"), sem("s_ln")
        s_x1d = sem("s_x1d")
        s_x1t, s_x1hi, s_x1lo = sem("s_x1t"), sem("s_x1hi"), sem("s_x1lo")
        s_rc = sem("s_rc")
        s_wr, s_wrs, s_rp, s_rt, s_ra = sem("s_wr"), sem("s_wrs"), sem("s_rp"), sem("s_rt"), sem("s_ra")
        s_rb = sem("s_rb")
        s_cho, s_pos, s_most = sem("s_cho"), sem("s_pos"), sem("s_most")
        s_tb, s_tabp, s_rows = sem("s_tb"), sem("s_tabp"), sem("s_rows")
        s_pw, s_phi, s_plo, s_pp, s_pev = sem("s_pw"), sem("s_phi"), sem("s_plo"), sem("s_pp"), sem("s_pev")
        s_ew = [[sem(f"s_ew{a}{q}") for q in range(3)] for a in range(2)]
        s_ehi, s_elo, s_elo2, s_used = sem("s_ehi"), sem("s_elo"), sem("s_elo2"), sem("s_used")
        s_got = [sem(f"s_got{a}") for a in range(2)]
        s_put = [sem(f"s_put{a}") for a in range(2)]
        s_cg, s_cp = sem("s_cg"), sem("s_cp")
        s_xt, s_xh, s_xl = sem("s_xt"), sem("s_xh"), sem("s_xl")
        s_silu, s_h, s_th, s_hh, s_hl = sem("s_silu"), sem("s_h"), sem("s_th"), sem("s_hh"), sem("s_hl")
        s_outa, s_outv = sem("s_outa"), sem("s_outv")
        s_gw = [sem(f"s_gw{q}") for q in range(4)]
        s_pair = [sem(f"s_pair{t}") for t in range(NT)]
        s_ghi, s_glo, s_gp = sem("s_ghi"), sem("s_glo"), sem("s_gp")
        s_y0, s_r2, s_bn2, s_ve2, s_rs2, s_ln2 = [sem(n) for n in ("s_y0", "s_r2", "s_bn2", "s_ve2", "s_rs2", "s_ln2")]
        s_x2t, s_x2hi, s_x2lo = sem("s_x2t"), sem("s_x2hi"), sem("s_x2lo")
        s_sig, s_mix, s_out = sem("s_sig"), sem("s_mix"), sem("s_out")

        def kind(n):
            return (None, n) if n < SMALL else ((n - SMALL) // PIECES, (n - SMALL) % PIECES)

        def piece_no(g, j):
            return SMALL + g * PIECES + j

        def slot(m, n):
            return m[:, (n % 6) * PW:(n % 6 + 1) * PW].rearrange("p (k c) -> p k c", k=NK)

        GATE_E = 3
        RT_GROUP, RT_SECOND = 7, 22
        TB, TB_SEATS = 9, 4
        def group(m, q):
            return m[:, q * GW:(q + 1) * GW].rearrange("p (u c) -> p u c", u=4)

        OSLOT = [1, 2, 0, 1]
        ESLOT = [1, 0, 2]
        ORAW = [0, GW, 8192, 8192 + GW]
        EW = 3 * GW
        mine = res[:, :].rearrange("p (t c) -> p t c", t=NT)

        def expert_blocks(eng, run):
            run(0, 0)
            fullest = eng.value_load(most[0:1, 0:1], min_val=0, max_val=SEQ)
            with eng.If(fullest > P):
                with eng.Fori(1, BLOCKS) as b:
                    run(b, b * NE)

        def wait_count(eng, sem_, value):
            if isinstance(value, int) and value <= 0:
                return
            eng.wait_ge(sem_, value)
            if not isinstance(value, int) and eng in (nc.sync, nc.gpsimd):
                eng.sem_inc(s_idle, 1)

        def arrived(T, par):
            return 8 * (T - par) + 16

        block = ctx.enter_context(nc.Block())

        @block.sync
        def _(sp):
            for c in range(4):
                sp.dma_start(x_raw[:, 2 * c:2 * c + 2, :], d["xT"][:, 2 * c:2 * c + 2, :]).then_inc(s_x[c], 16)
                if c == 0:
                    sp.dma_start(raw[:, 0:PW], d["w_in"][0, :, :]).then_inc(s_raw[0], 16)
            sp.dma_start(w16[:, :, :], d["w16"]).then_inc(s_w16, 16)
            sp.dma_start(if_bias[:, :], d["if_bias"].partition_broadcast(P)).then_inc(s_const, 16)
            sp.dma_start(conv_wb[:, :, :], d["conv_wb"]).then_inc(s_const, 16)
            sp.dma_start(gn_half[:, :], d["gn_w"].partition_broadcast(P)).then_inc(s_const, 16)
            for n in range(1, NPIECE):
                if n >= RAWS:
                    sp.wait_ge(s_wlo, n - RAWS + 1)
                r = n % RAWS
                sp.dma_start(raw[:, r * PW:(r + 1) * PW], d["w_in"][n, :, :]).then_inc(s_raw[r], 16)
            sp.wait_ge(s_wlo, NPIECE)
            sp.wait_ge(s_mdist, 6)
            sp.wait_ge(s_col_v, 2)
            for q in range(4):
                sp.dma_start(raw[:, ORAW[q]:ORAW[q] + GW], d["w_out"][q, :, :]).then_inc(s_or[q], 16)
            sp.wait_ge(s_ya, NG)
            sp.dma_start(wr_raw, d["w_router"]).then_inc(s_wr, 16)
            sp.dma_start(p_raw, d["pT"]).then_inc(s_pw, 16)
            sp.wait_ge(s_ym, NG)
            for t in range(NT):
                sp.dma_start(mine[:, t, :], d["x"][t * P:(t + 1) * P, :]).then_inc(s_xn[t], 16)
            sp.dma_start(ln_g, d["ln1_g"].partition_broadcast(P)).then_inc(s_lnw, 16)
            sp.dma_start(ln_b, d["ln1_b"].partition_broadcast(P)).then_inc(s_lnw, 16)
            sp.dma_start(r_bias, d["r_bias"].partition_broadcast(P)).then_inc(s_rb, 16)
            sp.wait_ge(s_yt, NK)
            sp.dma_start(y_flat[:, 0:GW], d["ple_proj"]).then_inc(s_pw, 16)

            def load(T, e, par, q):
                src = d["w_exp"][bass.ds(e, 1), :, q * GW:(q + 1) * GW].rearrange("a p c -> p (a c)")
                sp.dma_start(raw[:, par * EW + q * GW:par * EW + (q + 1) * GW], src).then_inc(s_ew[par][q], 16)

            def run(b, base):
                if isinstance(b, int):
                    sp.wait_ge(s_olo, 2)
                    for q in range(3):
                        load(0, 0, 0, q)
                    for t in range(NT):
                        sp.wait_ge(s_ln, 2 * t + 2)
                        sp.dma_start(x1_dram[t * P:(t + 1) * P, :], mine[:, t, :]).then_inc(s_x1d, 16)
                    sp.dma_start(ln_g, d["ln2_g"].partition_broadcast(P)).then_inc(s_lnw2, 16)
                    sp.dma_start(ln_b, d["ln2_b"].partition_broadcast(P)).then_inc(s_lnw2, 16)
                    sp.wait_ge(s_plo, 2)
                    sp.wait_ge(s_wrs, 2)
                    for q in range(3):
                        load(1, 1, 1, q)
                else:
                    wait_count(sp, s_elo, 2 * base)
                    wait_count(sp, s_elo2, base)
                    for par in range(2):
                        for q in range(3):
                            load(base + par, par, par, q)
                with sp.Fori(0, NE // 2 - 1) as i:
                    for par in range(2):
                        T = base + 2 * i + par
                        for q in range(3):
                            wait_count(sp, *((s_elo, 2 * T + q + 1) if q < 2 else (s_elo2, T + 1)))
                            load(T + 2, 2 * i + par + 2, par, q)
                for par in range(2):
                    wait_count(sp, s_put[par], 8 * (base + NE))

            expert_blocks(sp, run)
            Z = NE
            for q in range(2):
                sp.dma_start(raw[:, 8192 + q * GW:8192 + (q + 1) * GW], d["ple_gate"][q, :, :]).then_inc(s_gw[q], 16)
            for t in range(NT):
                sp.dma_start(raw[:, t * 2 * DM:(t + 1) * 2 * DM].rearrange("p (k c) -> p k c", k=2),
                             pair_dram.rearrange("(k t p) c -> t p k c", k=2, p=P)[t, :, :, :]).then_inc(s_pair[t], 16)
            for q in range(2, 4):
                sp.dma_start(y_flat[:, (q - 2) * GW:(q - 1) * GW], d["ple_gate"][q, :, :]).then_inc(s_gw[q], 16)
            for u in range(2 * NT):
                half, t = u // NT, u % NT
                sp.wait_ge(s_mix, 2 * u + 2)
                sp.dma_start(out[t * P:(t + 1) * P, half * 512:(half + 1) * 512],
                             raw[:, t * DM + half * 512:t * DM + (half + 1) * 512]).then_inc(s_out, 16)
            sp.wait_ge(s_out, 16 * 2 * NT)

        @block.gpsimd
        def _(pool):
            g = nc.gpsimd
            g.memset(ident[:, :], 0.0).then_inc(s_setup, 1)
            g.memset(sel_head[:, :, :], 0.0).then_inc(s_setup, 1)
            g.memset(minus_half, -0.5).then_inc(s_setup, 1)
            for grp in range(NG):
                pool.wait_ge(s_setup, 3 + 2 * grp)
                g.memset(q_scale[0:DA, grp:grp + 1], 2.0 ** (2 * grp - 2)).then_inc(s_setup, 1)
                pool.wait_ge(s_setup, 4 + 2 * grp)
                g.memset(q_scale[DA:P, grp:grp + 1], 2.0 ** (2 * grp - 1)).then_inc(s_setup, 1)
            pool.wait_ge(s_setup, 11)
            g.memset(v_m[:, :, :, P:P + 1], 1.0).then_inc(s_setup, 1)
            g.memset(pre[:, :, 0:3], 0.0).then_inc(s_setup, 1)
            g.iota(dist[:, :], pattern=[[-1, SEQ]], base=384, channel_multiplier=1,
                   allow_small_or_imprecise_dtypes=True).then_inc(s_setup, 1)
            pool.wait_ge(s_setup, 14)
            g.affine_select(out=ident[:, :], in_=ident[:, :], compare_op=ALU.not_equal, fill=1.0, base=0,
                            pattern=[[-1, P]], channel_multiplier=1).then_inc(s_setup, 1)
            g.affine_select(out=sel_head[:, :, :], in_=sel_head[:, :, :], compare_op=ALU.not_equal, fill=1.0,
                            base=0, pattern=[[-1, HM], [0, P]], channel_multiplier=1).then_inc(s_setup, 1)
            g.affine_select(out=mdist[:, 0:P], in_=dist[:, 384:512], compare_op=ALU.is_ge, fill=BIG, base=0,
                            pattern=[[-1, P]], channel_multiplier=1).then_inc(s_md0, 1)

            def split(n):
                pool.wait_ge(s_whi, n + 1)
                r = n % RAWS
                g.tensor_tensor(w_lo[:, (n % 6) * PW:(n % 6 + 1) * PW], raw[:, r * PW:(r + 1) * PW],
                                w_hi[:, (n % 6) * PW:(n % 6 + 1) * PW].bitcast(F32), ALU.subtract)\
                    .then_inc(s_wlo, 1)

            def strike_future():
                for b in range(1, NT):
                    pool.wait_ge(s_acc, HI_ * b)
                    last = score[:, SO[b] + b * P:SO[b] + (b + 1) * P]
                    g.affine_select(out=last, in_=last, compare_op=ALU.is_ge, fill=-BIG, base=0,
                                    pattern=[[-1, P]], channel_multiplier=1).then_inc(s_fut, 1)

            def mask_decay(h):
                pool.wait_ge(s_dexp, h + 1)
                for b in range(NT):
                    own = decay[:, LO_[b]:LO_[b] + P]
                    g.affine_select(out=own, in_=own, compare_op=ALU.is_ge, fill=0.0, base=0,
                                    pattern=[[1, P]], channel_multiplier=-1).then_inc(s_dmask, 1)

            def power(h):
                pool.wait_ge(s_var, h + 1)
                g.tensor_tensor(rstd, den, minus_half, ALU.pow).then_inc(s_pow, 1)

            for n in range(6):
                split(n)
            for n in range(NPIECE):
                if n + 6 < NPIECE:
                    split(n + 6)
                if n == SMALL:
                    strike_future()
                grp, j = kind(n)
                if grp and j == 0:
                    mask_decay(grp - 1)
                if grp and j == 6:
                    power(grp - 1)
            def split_out(q):
                pool.wait_ge(s_ohi, q + 1)
                g.tensor_tensor(group(w_lo, OSLOT[q]), raw[:, ORAW[q]:ORAW[q] + GW].rearrange("p (u c) -> p u c", u=4),
                                group(w_hi, OSLOT[q]).bitcast(F32), ALU.subtract).then_inc(s_olo, 1)

            mask_decay(NG - 1)
            split_out(0)
            split_out(1)
            power(NG - 1)
            split_out(2)
            pool.wait_ge(s_ym, NG)
            g.memset(tri[:, :], 1.0).then_inc(s_rc, 1)
            g.memset(ones[:, :], 1.0).then_inc(s_rc, 1)
            flags = dict(allow_small_or_imprecise_dtypes=True)
            g.iota(count_c, pattern=[[1, P]], base=0, channel_multiplier=0, **flags).then_inc(s_rc, 1)
            g.iota(rank, pattern=[[-1, EG]], base=EG, channel_multiplier=0, **flags).then_inc(s_rc, 1)
            g.iota(token, pattern=[[P, NT]], base=0, channel_multiplier=1, **flags).then_inc(s_rc, 1)
            g.iota(skip_row, pattern=[[1, 1]], base=SKIP, channel_multiplier=1, **flags).then_inc(s_rc, 1)
            pool.wait_ge(s_rc, 6)
            g.affine_select(out=tri[:, :], in_=tri[:, :], compare_op=ALU.is_gt, fill=0.0, base=0,
                            pattern=[[1, P]], channel_multiplier=-1).then_inc(s_rc, 1)
            split_out(3)
            pool.wait_ge(s_ve, 1)
            g.tensor_tensor(rs8, ve8, minus_half, ALU.pow).then_inc(s_rs, 1)
            pool.wait_ge(s_phi, 1)
            g.tensor_tensor(a_lo[:, 0:2, :], p_raw, a_hi[:, 0:2, :].bitcast(F32), ALU.subtract).then_inc(s_plo, 1)
            pool.wait_ge(s_phi, 2)
            g.tensor_tensor(w_lo[:, 0:GW], y_flat[:, 0:GW], w_hi[:, 0:GW].bitcast(F32), ALU.subtract)\
                .then_inc(s_plo, 1)

            def gather(T, e, par):
                g.tensor_copy(at_got[:, par:par + 1], row_got[:, bass.ds(e, 1)]).then_inc(s_cg, 1)
                wait_count(pool, s_cg, T + 1)
                g.indirect_dma_start(out=x_got[par], out_offset=None, in_=x1_dram[:, :],
                                     in_offset=bass.IndirectOffsetOnAxis(ap=at_got[:, par:par + 1], axis=0),
                                     bounds_check=SEQ - 1, oob_is_err=False).then_inc(s_got[par], 16)

            def scatter(T, e, par):
                wait_count(pool, s_put[par], arrived(T - 2, par))
                g.tensor_copy(at_put[:, par:par + 1], row_put[:, bass.ds(e, 1)]).then_inc(s_cp, 1)
                wait_count(pool, s_cp, T + 1)
                wait_count(pool, s_outa, T + 1)
                wait_count(pool, s_outv, T + 1)
                g.indirect_dma_start(out=pair_dram[:, :],
                                     out_offset=bass.IndirectOffsetOnAxis(ap=at_put[:, par:par + 1], axis=0),
                                     in_=y_out[par], in_offset=None,
                                     bounds_check=2 * SEQ - 1, oob_is_err=False).then_inc(s_put[par], 16)

            def split_down(T, par):
                wait_count(pool, s_ehi, 3 * T + 3)
                at_ = par * EW + 2 * GW
                g.tensor_tensor(w_lo[:, ESLOT[2] * GW:(ESLOT[2] + 1) * GW], raw[:, at_:at_ + GW],
                                w_hi[:, ESLOT[2] * GW:(ESLOT[2] + 1) * GW].bitcast(F32), ALU.subtract)\
                    .then_inc(s_elo2, 1)

            def run(b, base):
                wait_count(pool, s_rows, 2 * b + 2)
                if isinstance(b, int):
                    pool.wait_ge(s_x1d, 16 * NT)
                for par in range(2):
                    gather(base + par, par, par)
                split_down(base, 0)

                def pair(i, last):
                    for par in range(2):
                        T = base + 2 * i + par
                        if not last:
                            wait_count(pool, s_xt, 2 * T + 2)
                            gather(T + 2, 2 * i + par + 2, par)
                        if not (last and par):
                            split_down(T + 1, 1 - par)
                        scatter(T, 2 * i + par, par)

                pair(0, False)
                with pool.Fori(1, NE // 2 - 1) as i:
                    pair(i, False)
                pair(NE // 2 - 1, True)
                for par in range(2):
                    wait_count(pool, s_put[par], 8 * (base + NE))

            expert_blocks(pool, run)

            def split_gate(q):
                pool.wait_ge(s_ghi, q + 1)
                src = raw[:, 8192 + q * GW:8192 + (q + 1) * GW] if q < 2 else y_flat[:, (q - 2) * GW:(q - 1) * GW]
                g.tensor_tensor(group(w_lo, OSLOT[q]), src.rearrange("p (u c) -> p u c", u=4),
                                group(w_hi, OSLOT[q]).bitcast(F32), ALU.subtract).then_inc(s_glo, 1)

            split_gate(0)
            split_gate(1)
            split_gate(2)
            pool.wait_ge(s_ve2, 1)
            g.tensor_tensor(rs8, ve8, minus_half, ALU.pow).then_inc(s_rs2, 1)
            split_gate(3)

        @block.scalar
        def _(act):
            a = nc.scalar

            def round_piece(n):
                if n >= 6:
                    act.wait_ge(s_proj, n - 5)
                r = n % RAWS
                act.wait_ge(s_raw[r], 16 * (n // RAWS + 1))
                a.activation(w_hi[:, (n % 6) * PW:(n % 6 + 1) * PW], raw[:, r * PW:(r + 1) * PW], ACT.Copy)\
                    .then_inc(s_whi, 1)

            def evacuate(n):
                act.wait_ge(s_proj, n + 1)
                grp, j = kind(n)
                src = proj_bank[n % 2]
                tiles = src[:, :].rearrange("p (s c) -> p s c", s=NT)
                if grp is None:
                    a.activation(qi[:, j, :] if j < 2 else ki, src[:, :], ACT.Copy).then_inc(s_evac, 1)
                    return
                par = grp % 2
                if j == 0:
                    if grp >= 2:
                        act.wait_ge(s_qk, 8 * (grp - 1))
                    if grp == 0:
                        act.wait_ge(s_setup, 14)
                    a.activation(q_t[:, par, :], src[:, :], ACT.Identity, scale=q_scale[:, grp:grp + 1])\
                        .then_inc(s_evac, 1)
                elif j == 1:
                    a.activation(k_t[:, par, :], src[:, :], ACT.Copy).then_inc(s_evac, 1)
                elif j == 2:
                    if grp >= 2:
                        act.wait_ge(s_pv, 8 * (grp - 1))
                    a.activation(v_a[:, par, :, :], tiles, ACT.Copy).then_inc(s_evac, 1)
                elif j in (3, 4):
                    if grp >= 1:
                        act.wait_ge(s_cacc, 8 * grp)
                    a.activation(pre[:, j - 3, 3:515], src[:, :], ACT.Copy).then_inc(s_evac, 1)
                elif j == 5:
                    if grp >= 2:
                        act.wait_ge(s_mnum, grp - 1)
                    a.activation(v_m[:, par, :, 0:P], tiles, ACT.Copy).then_inc(s_evac, 1)
                else:
                    if grp >= 2:
                        act.wait_ge(s_ym, grp - 1)
                    a.activation(o_m[:, par, :, :], tiles, ACT.Tanh, scale=0.5).then_inc(s_evac, 1)

            def gates():
                act.wait_ge(s_row_v, 3)
                a.activation(c_row, c_row, ACT.Exp, scale=-1.0).then_inc(s_row_a, 1)
                act.wait_ge(s_row_a, 1)
                a.activation(c_row, c_row, ACT.Ln, bias=1.0).then_inc(s_row_a, 1)
                act.wait_ge(s_row_v, 10)
                a.activation(g_row, c_row, ACT.Exp, scale=-1.0).then_inc(s_row_a, 1)

            def index_relu():
                for n in range(3 * HI_):
                    b, h = n // HI_ + 1, n % HI_
                    act.wait_ge(s_idx, n + 1)
                    if n >= 2:
                        act.wait_ge(s_acc, n - 1)
                    a.activation(relu[:, n % 2, 0:(b + 1) * P], score_bank[n % 2][:, 0:(b + 1) * P], ACT.Relu,
                                 scale=DI ** -0.5).then_inc(s_relu, 1)

            def softmax(g, u):
                U, h, b = 8 * g + u, 2 * g + u // NT, u % NT
                act.wait_ge(s_negmax, U + 1)
                if U >= 2:
                    act.wait_ge(s_turn, U - 1)
                if u == 0 and g >= 1:
                    act.wait_ge(s_yinv, g)
                a.activation(prob[:, U % 2, 0:(b + 1) * P], masked[:, U % 2, 0:(b + 1) * P], ACT.Exp,
                             scale=2.0 ** -(h + 1), bias=neg_max[:, U % 2:U % 2 + 1],
                             accum_out=row_sum[:, b, u // NT:u // NT + 1]).then_inc(s_exp, 1)

            def lstm_exp(h):
                act.wait_ge(s_gadd, 4 * (h + 1))
                a.activation(decay[:, :], decay[:, :], ACT.Exp).then_inc(s_dexp, 1)

            def lstm_hidden(h):
                act.wait_ge(s_mnum, h + 1)
                if h >= 1:
                    act.wait_ge(s_ym, h)
                for half in range(2):
                    a.activation(hidden[:, 2 * half:2 * half + 2, :],
                                 lstm_bank[half][:, 0:258].rearrange("p (s c) -> p s c", s=2), ACT.Copy)\
                        .then_inc(s_hid, 1)

            def conv_tanh(h, c):
                act.wait_ge(s_cacc, 8 * h + 4 * c + 4)
                if 2 * h + c >= 1:
                    act.wait_ge(s_conv, 2 * h + c)
                a.activation(tanh_c, conv[:, c, :], ACT.Tanh, scale=0.5).then_inc(s_ctanh, 1)

            def slot_work(g, j):
                if j == 0:
                    lstm_exp(g)
                if j < 4:
                    softmax(g, 2 * j)
                    softmax(g, 2 * j + 1)
                if j == 6:
                    lstm_hidden(g)

            def round_x(c):
                act.wait_ge(s_x[c], 16)
                a.activation(a_hi[:, 2 * c:2 * c + 2, :], x_raw[:, 2 * c:2 * c + 2, :], ACT.Copy).then_inc(s_xhi, 1)

            round_x(0)
            round_piece(0)
            round_x(1)
            round_x(2)
            round_x(3)
            act.wait_ge(s_w16, 16)
            a.activation(w16_hi[:, :, :], w16[:, :, :], ACT.Copy).then_inc(s_w16s, 1)
            for n in range(1, 6):
                round_piece(n)
            for n in range(NPIECE):
                grp, j = kind(n)
                if n == SMALL:
                    gates()
                    index_relu()
                evacuate(n)
                if n + 6 < NPIECE:
                    round_piece(n + 6)
                if grp:
                    slot_work(grp - 1, j)
                if grp is not None and j >= 5:
                    conv_tanh(grp, j - 5)
            def round_out(q):
                act.wait_ge(s_or[q], 16)
                if q < 3:
                    act.wait_ge(s_proj, [28, 30, 31][q])
                else:
                    act.wait_ge(s_wo, 1)
                a.activation(group(w_hi, OSLOT[q]), raw[:, ORAW[q]:ORAW[q] + GW].rearrange("p (u c) -> p u c", u=4),
                             ACT.Copy).then_inc(s_ohi, 1)

            for j in range(PIECES):
                slot_work(NG - 1, j)
                if j in (1, 3, 5):
                    round_out(j // 2)
            for k in range(NK):
                act.wait_ge(s_yt, k + 1)
                a.activation(a_hi[:, k, :], bank[k % 4][:, :], ACT.Copy).then_inc(s_yhi, 1)
            round_out(3)
            act.wait_ge(s_wr, 16)
            act.wait_ge(s_wo, 2)
            a.activation(w_hi[:, WR_AT:3 * GW], wr_raw.rearrange("p k c -> p (k c)"), ACT.Copy).then_inc(s_wrs, 1)
            for u in range(2 * NT):
                t, half = u // 2, u % 2
                act.wait_ge(s_x1t, u + 1)
                a.activation(a_hi[:, 4 * half:4 * half + 4, t * P:(t + 1) * P],
                             bank[u % 4][:, :].rearrange("p (k c) -> p k c", k=4), ACT.Copy).then_inc(s_x1hi, 1)
            act.wait_ge(s_pw, 32)
            act.wait_ge(s_rp, 1)
            a.activation(a_hi[:, 0:2, :], p_raw, ACT.Copy).then_inc(s_phi, 1)
            act.wait_ge(s_wo, 3)
            a.activation(w_hi[:, 0:GW], y_flat[:, 0:GW], ACT.Copy).then_inc(s_phi, 1)
            act.wait_ge(s_rt, RT_GROUP)
            a.activation(dif_g, dif_g, ACT.Exp).then_inc(s_ra, 1)
            act.wait_ge(s_rt, RT_SECOND)
            a.activation(col[5], col[5], ACT.Exp).then_inc(s_ra, 1)

            def round_expert(T, par, q, first=False):
                act.wait_ge(s_ew[par][q], arrived(T, par))
                if first:
                    act.wait_ge(*[(s_wo, 4), (s_pp, 2 * NT), (s_rp, 1)][q])
                else:
                    act.wait_ge(s_used, 3 * T - 2 + q)
                a.activation(group(w_hi, ESLOT[q]),
                             raw[:, par * EW + q * GW:par * EW + (q + 1) * GW].rearrange("p (u c) -> p u c", u=4),
                             ACT.Copy).then_inc(s_ehi, 1)

            def ple_out(u):
                act.wait_ge(s_pp, u + 1)
                a.activation(ple[:, u // 2, (u % 2) * 512:(u % 2 + 1) * 512], bank[u % 4][:, :], ACT.Copy)\
                    .then_inc(s_pev, 1)

            def tokens_hi(T, par, half):
                act.wait_ge(s_xt, 2 * T + half + 1)
                a.activation(xg(hi_flat, par)[:, 4 * half:4 * half + 4, :],
                             bank[2 + half][:, :].rearrange("p (k c) -> p k c", k=4), ACT.Copy).then_inc(s_xh, 1)

            round_expert(0, 0, 0, True)
            for u in range(2 * NT):
                ple_out(u)

            def run(b, base):
                if isinstance(b, int):
                    round_expert(0, 0, 1, True)
                    round_expert(0, 0, 2, True)
                else:
                    for q in range(3):
                        round_expert(base, 0, q)
                for half in range(2):
                    tokens_hi(base, 0, half)

                def expert(T, par, last):
                    if not last:
                        round_expert(T + 1, 1 - par, 0)
                    act.wait_ge(s_used, 3 * T + 2)
                    a.activation(silu_g, bank[0][:, 0:DE], ACT.Silu).then_inc(s_silu, 1)
                    if not last:
                        tokens_hi(T + 1, 1 - par, 0)
                    act.wait_ge(s_th, T + 1)
                    a.activation(ht(hi_flat), bank[1][:, 0:DE].rearrange("p (k c) -> p k c", k=2), ACT.Copy)\
                        .then_inc(s_hh, 1)
                    if not last:
                        tokens_hi(T + 1, 1 - par, 1)
                        round_expert(T + 1, 1 - par, 1)
                    act.wait_ge(s_used, 3 * T + 3)
                    wait_count(act, s_put[par], arrived(T - 2, par))
                    a.activation(y_out[par][:, 0:512], bank[4][:, :], ACT.Copy).then_inc(s_outa, 1)
                    if not last:
                        round_expert(T + 1, 1 - par, 2)

                for par in range(2):
                    expert(base + par, par, False)
                with act.Fori(1, NE // 2 - 1) as i:
                    for par in range(2):
                        expert(base + 2 * i + par, par, False)
                for par in range(2):
                    expert(base + NE - 2 + par, par, par == 1)
                for par in range(2):
                    act.wait_ge(s_put[par], 8 * (base + NE))

            expert_blocks(act, run)

            def round_gate(q):
                act.wait_ge(s_gw[q], 16)
                if q == 3:
                    act.wait_ge(s_gp, 1)
                src = raw[:, 8192 + q * GW:8192 + (q + 1) * GW] if q < 2 else y_flat[:, (q - 2) * GW:(q - 1) * GW]
                a.activation(group(w_hi, OSLOT[q]), src.rearrange("p (u c) -> p u c", u=4), ACT.Copy)\
                    .then_inc(s_ghi, 1)

            round_gate(0)
            for t in range(NT):
                act.wait_ge(s_pair[t], 16)
                first = raw[:, t * 2 * DM:t * 2 * DM + DM]
                a.activation(first, first, ACT.Copy, scale=gate_w[0][:, t:t + 1]).then_inc(s_y0, 1)
            round_gate(1)
            round_gate(2)
            for u in range(2 * NT):
                t, half = u // 2, u % 2
                act.wait_ge(s_x2t, u + 1)
                a.activation(a_hi[:, 4 * half:4 * half + 4, t * P:(t + 1) * P],
                             bank[u % 4][:, :].rearrange("p (k c) -> p k c", k=4), ACT.Copy).then_inc(s_x2hi, 1)
            round_gate(3)
            for u in range(2 * NT):
                half, t = u // NT, u % NT
                act.wait_ge(s_gp, 2 * half + 2)
                a.activation(raw[:, t * DM + half * 512:t * DM + (half + 1) * 512],
                             bank[4 * (1 - half) + t][:, :], ACT.Sigmoid).then_inc(s_sig, 1)

        @block.vector
        def _(dve):
            v = nc.vector
            for c in range(4):
                dve.wait_ge(s_xhi, c + 1)
                v.tensor_tensor(a_lo[:, 2 * c:2 * c + 2, :], x_raw[:, 2 * c:2 * c + 2, :],
                                a_hi[:, 2 * c:2 * c + 2, :].bitcast(F32), ALU.subtract).then_inc(s_xlo, 1)
            dve.wait_ge(s_w16s, 1)
            v.tensor_tensor(w16_lo[:, :, :], w16[:, :, :], w16_hi[:, :, :].bitcast(F32), ALU.subtract)\
                .then_inc(s_w16s, 1)

            def gates():
                dve.wait_ge(s_gate_p, 1)
                pre16 = lstm_bank[0][:, 0:64].rearrange("p (s c) -> p s c", s=NT)
                v.tensor_scalar(w_head[:, :, :], pre16[:, :, 0:8], HI_ ** -0.5, None, ALU.mult).then_inc(s_gate_e, 1)
                dve.wait_ge(s_const, 48)
                v.tensor_tensor(if_pre[:, :, :], pre16[:, :, 8:16],
                                if_bias[:, :].unsqueeze(1).broadcast_to([P, NT, 8]), ALU.add).then_inc(s_gate_e, 1)
                v.tensor_scalar(gn_half[:, :], gn_half[:, :], 0.5, None, ALU.mult).then_inc(s_gate_e, 1)
                dve.wait_ge(s_row_p, 1)
                v.tensor_copy(i_row, lstm_bank[1][0:HM, :]).then_inc(s_row_v, 1)
                v.tensor_copy(f_row, turn_bank[0:HM, :]).then_inc(s_row_v, 1)
                dve.wait_ge(s_row_v, 2)
                v.scalar_tensor_tensor(out=c_row, in0=f_row, scalar=-1.0, in1=f_row, op0=ALU.mult,
                                       op1=ALU.max).then_inc(s_row_v, 1)
                v.memset(g_row, 1.0).then_inc(s_row_v, 1)
                dve.wait_ge(s_row_a, 2)
                v.scalar_tensor_tensor(out=f_row, in0=f_row, scalar=0.0, in1=c_row, op0=ALU.min,
                                       op1=ALU.subtract).then_inc(s_row_v, 1)
                dve.wait_ge(s_row_v, 5)
                v.tensor_tensor_scan(c_row, g_row, f_row, 0.0, ALU.mult, ALU.add).then_inc(s_row_v, 1)
                dve.wait_ge(s_row_v, 6)
                v.tensor_tensor(i_row, i_row, c_row, ALU.subtract).then_inc(s_row_v, 1)
                dve.wait_ge(s_row_v, 7)
                v.tensor_tensor_scan(g_row, i_row, i_row, 0.0, ALU.max, ALU.max).then_inc(s_row_v, 1)
                dve.wait_ge(s_row_v, 8)
                v.tensor_tensor(c_row, c_row, g_row, ALU.add).then_inc(s_row_v, 1)
                v.tensor_scalar(nega_row, g_row, -1.0, None, ALU.mult).then_inc(s_row_v, 1)
                dve.wait_ge(s_col_p, 2)
                cols = lstm_bank[0][:, 0:32].rearrange("p (k s h) -> p k s h", k=2, s=NT)
                v.tensor_copy(a_col[:, :, :], cols[:, 0, :, :]).then_inc(s_col_v, 1)
                v.tensor_copy(em_col[:, :, :], cols[:, 1, :, :]).then_inc(s_col_v, 1)

            def index_sum():
                for n in range(3 * HI_):
                    b, h = n // HI_ + 1, n % HI_
                    dve.wait_ge(s_relu, n + 1)
                    acc = score[:, SO[b]:SO[b] + (b + 1) * P]
                    w = w_head[:, b, h:h + 1]
                    r = relu[:, n % 2, 0:(b + 1) * P]
                    if h == 0:
                        v.tensor_scalar(acc, r, w, None, ALU.mult).then_inc(s_acc, 1)
                    else:
                        dve.wait_ge(s_acc, n)
                        v.scalar_tensor_tensor(out=acc, in0=r, scalar=w, in1=acc, op0=ALU.mult, op1=ALU.add)\
                            .then_inc(s_acc, 1)

            def top_keys():
                dve.wait_ge(s_fut, 3)
                n = 0
                for r in range(TOPK // 8):
                    for b in range(1, NT):
                        src = (score if r == 0 else left)[:, SO[b]:SO[b] + (b + 1) * P]
                        if r:
                            dve.wait_ge(s_top, 6 * (r - 1) + 3 + b)
                        v.max(best[:, b - 1, :], src).then_inc(s_top, 1)
                    for b in range(1, NT):
                        src = (score if r == 0 else left)[:, SO[b]:SO[b] + (b + 1) * P]
                        dve.wait_ge(s_top, 6 * r + b)
                        v.match_replace(left[:, SO[b]:SO[b] + (b + 1) * P], best[:, b - 1, :], src, TAKEN)\
                            .then_inc(s_top, 1)
                dve.wait_ge(s_top, 6 * (TOPK // 8))
                for b in range(1, NT):
                    part = left[:, SO[b]:SO[b] + (b + 1) * P]
                    v.tensor_scalar(part, part, TAKEN / 10, BIG, ALU.is_ge, ALU.mult).then_inc(s_mdist, 1)
                for b in range(1, NT):
                    dve.wait_ge(s_mdist, b)
                    v.tensor_tensor(mdist[:, MO[b]:MO[b] + (b + 1) * P], left[:, SO[b]:SO[b] + (b + 1) * P],
                                    dist[:, (3 - b) * P:SEQ], ALU.add).then_inc(s_mdist, 1)
                dve.wait_ge(s_md0, 1)
                dve.wait_ge(s_mdist, 6)

            def mask_scores(g, u):
                U, h, b = 8 * g + u, 2 * g + u // NT, u % NT
                dve.wait_ge(s_qk, U + 1)
                if U >= 2:
                    dve.wait_ge(s_exp, U - 1)
                n = (b + 1) * P
                v.tensor_tensor_reduce(out=masked[:, U % 2, 0:n], in0=score_bank[U % 2][:, 0:n],
                                       in1=mdist[:, MO[b]:MO[b] + n], scale=1.0, scalar=-3.0e38,
                                       op0=ALU.subtract, op1=ALU.max,
                                       accum_out=row_max[:, U % 2:U % 2 + 1]).then_inc(s_masked, 1)
                dve.wait_ge(s_masked, U + 1)
                v.tensor_scalar(neg_max[:, U % 2:U % 2 + 1], row_max[:, U % 2:U % 2 + 1], -(2.0 ** -(h + 1)), None,
                                ALU.mult).then_inc(s_negmax, 1)

            def copy_turned(g, u):
                U, n = 8 * g + u, (u % NT + 1) * P
                dve.wait_ge(s_turn, U + 1)
                if U >= 2:
                    dve.wait_ge(s_pv, U - 1)
                v.tensor_copy(prob_t[:, U % 2, 0:n], turn_bank[:, 0:n]).then_inc(s_probt, 1)

            def attn_out(g):
                dve.wait_ge(s_pv, 8 * (g + 1))
                dve.wait_ge(s_exp, 8 * (g + 1))
                if g:
                    dve.wait_ge(s_ya, g)
                v.reciprocal(row_inv, row_sum).then_inc(s_yinv, 1)
                dve.wait_ge(s_yinv, g + 1)
                v.tensor_tensor(y[:, :, g * P:(g + 1) * P].rearrange("p t (h c) -> p t h c", h=2),
                                attn_bank[:, :].rearrange("p (t h c) -> p t h c", t=NT, h=2),
                                row_inv.unsqueeze(3).broadcast_to([P, NT, 2, DA]), ALU.mult).then_inc(s_ya, 1)

            def lstm_add(h):
                dve.wait_ge(s_gbc, h + 1)
                if h:
                    dve.wait_ge(s_mw, 4 * h)
                else:
                    dve.wait_ge(s_xlo, 4)
                for b in range(NT):
                    v.tensor_scalar(decay[:, LO_[b]:LO_[b + 1]], lstm_bank[1][:, b * P:SEQ],
                                    a_col[:, b, h:h + 1], 0.0, ALU.add, ALU.min).then_inc(s_gadd, 1)

            def lstm_weight(h, b):
                dve.wait_ge(s_mqk, 4 * h + b + 1)
                dve.wait_ge(s_dmask, 4 * (h + 1))
                if h:
                    dve.wait_ge(s_mnum, h)
                v.scalar_tensor_tensor(out=weight[:, LO_[b]:LO_[b + 1]],
                                       in0=lstm_bank[b % 2][:, 0:SEQ - b * P], scalar=0.25 * P ** -0.5,
                                       in1=decay[:, LO_[b]:LO_[b + 1]], op0=ALU.mult, op1=ALU.mult)\
                    .then_inc(s_mw, 1)

            def convolve(h, c):
                w = conv_wb[:, 4 * c + h, :]
                dve.wait_ge(s_evac, piece_no(h, 3 + c) + 1)
                n = 8 * h + 4 * c
                if 2 * h + c >= 2:
                    dve.wait_ge(s_conv, 2 * h + c - 1)
                v.tensor_scalar(conv[:, c, :], pre[:, c, 0:SEQ], w[:, 0:1], w[:, 4:5], ALU.mult, ALU.add)\
                    .then_inc(s_cacc, 1)
                for tap in range(1, 4):
                    dve.wait_ge(s_cacc, n + tap)
                    v.scalar_tensor_tensor(out=conv[:, c, :], in0=pre[:, c, tap:tap + SEQ], scalar=w[:, tap:tap + 1],
                                           in1=conv[:, c, :], op0=ALU.mult, op1=ALU.add).then_inc(s_cacc, 1)
                dve.wait_ge(s_ctanh, 2 * h + c + 1)
                if h:
                    dve.wait_ge(s_mqk, 4 * h)
                v.scalar_tensor_tensor(out=qk_m[:, c, :], in0=tanh_c, scalar=1.0, in1=conv[:, c, :], op0=ALU.add,
                                       op1=ALU.mult).then_inc(s_conv, 1)

            POST = 17

            def lstm_out(h):
                n = [POST * h]

                def step(ins):
                    n[0] += 1
                    ins.then_inc(s_post, 1)

                def settle():
                    dve.wait_ge(s_post, n[0])

                dve.wait_ge(s_hid, 2 * (h + 1))
                if h:
                    dve.wait_ge(s_pow, h)
                raw_den = hidden[:, :, P:P + 1].squeeze(2)
                step(v.scalar_tensor_tensor(out=den, in0=raw_den, scalar=-1.0, in1=raw_den, op0=ALU.mult,
                                            op1=ALU.max))
                settle()
                step(v.tensor_tensor(den, den, em_col[:, :, h], ALU.max))
                settle()
                step(v.reciprocal(den_inv, den))
                settle()
                hid = hidden[:, :, 0:P]
                step(v.tensor_tensor(hid, hid, den_inv.unsqueeze(2).broadcast_to([P, NT, P]), ALU.mult))
                settle()
                for t in range(NT):
                    step(v.bn_stats(stats[:, t, :], hid[:, t, :]))
                settle()
                for t in range(NT):
                    step(v.bn_aggr(mean_var[:, t, :], stats[:, t, :]))
                settle()
                v.tensor_scalar(den, mean_var[:, :, 1:2].squeeze(2), EPS, None, ALU.add).then_inc(s_var, 1)
                dve.wait_ge(s_pow, h + 1)
                for t in range(NT):
                    step(v.tensor_scalar(hid[:, t, :], hid[:, t, :], mean_var[:, t, 0:1], rstd[:, t:t + 1],
                                         ALU.subtract, ALU.mult))
                settle()
                step(v.tensor_tensor(hid, hid, gn_half[:, h * P:(h + 1) * P].unsqueeze(1).broadcast_to([P, NT, P]),
                                     ALU.mult))
                settle()
                assert n[0] == POST * (h + 1), n
                v.scalar_tensor_tensor(out=y[:, :, (4 + h) * P:(5 + h) * P], in0=o_m[:, h % 2, :, :], scalar=1.0,
                                       in1=hid, op0=ALU.add, op1=ALU.mult).then_inc(s_ym, 1)

            def slot_work(g, j):
                if j == 0:
                    lstm_add(g)
                for e in range(2):
                    if j < 4:
                        mask_scores(g, 2 * j + e)
                    if 1 <= j <= 4:
                        copy_turned(g, 2 * j - 2 + e)
                if 1 <= j <= 4:
                    lstm_weight(g, j - 1)
                if j == 5:
                    attn_out(g)
                if j == 6:
                    lstm_out(g)

            gates()
            index_sum()
            top_keys()
            dve.wait_ge(s_gate_e, GATE_E)
            for g in range(NG):
                for j in range(PIECES):
                    if g:
                        slot_work(g - 1, j)
                    if j >= 5:
                        convolve(g, j - 5)
            for j in range(PIECES):
                slot_work(NG - 1, j)
            for k in range(NK):
                dve.wait_ge(s_yhi, k + 1)
                v.tensor_tensor(a_lo[:, k, :], bank[k % 4][:, :], a_hi[:, k, :].bitcast(F32), ALU.subtract)\
                    .then_inc(s_ylo, 1)
            for half in range(2):
                dve.wait_ge(s_wo, 2 * half + 2)
                for t in range(NT):
                    if half == 0:
                        dve.wait_ge(s_xn[t], 16)
                    r = mine[:, t, half * 512:(half + 1) * 512]
                    v.scalar_tensor_tensor(out=r, in0=r, scalar=ALPHA, in1=bank[4 * (1 - half) + t][:, :],
                                           op0=ALU.mult, op1=ALU.add).then_inc(s_r, 1)

            def norm_stats(ready, count, done):
                for t in range(NT):
                    for half in range(2):
                        v.bn_stats(stat8[:, t, 6 * half:6 * half + 6], mine[:, t, half * 512:(half + 1) * 512])\
                            .then_inc(count, 1)
                dve.wait_ge(count, 2 * NT)
                for t in range(NT):
                    v.bn_aggr(mv8[:, t, :], stat8[:, t, :]).then_inc(count, 1)
                dve.wait_ge(count, 3 * NT)
                v.tensor_scalar(ve8, mv8[:, :, 1:2].squeeze(2), EPS, None, ALU.add).then_inc(done, 1)

            def norm_apply(t, done):
                m = mine[:, t, :]
                v.scalar_tensor_tensor(out=m, in0=m, scalar=mv8[:, t, 0:1], in1=ln_g, op0=ALU.subtract,
                                       op1=ALU.mult).then_inc(done, 1)
                dve.wait_ge(done, 2 * t + 1)
                v.scalar_tensor_tensor(out=m, in0=m, scalar=rs8[:, t:t + 1], in1=ln_b, op0=ALU.mult,
                                       op1=ALU.add).then_inc(done, 1)

            def turned_low(u, hi, lo):
                t, half = u // 2, u % 2
                dve.wait_ge(hi, u + 1)
                v.tensor_tensor(a_lo[:, 4 * half:4 * half + 4, t * P:(t + 1) * P],
                                bank[u % 4][:, :].rearrange("p (k c) -> p k c", k=4),
                                a_hi[:, 4 * half:4 * half + 4, t * P:(t + 1) * P].bitcast(F32), ALU.subtract)\
                    .then_inc(lo, 1)

            dve.wait_ge(s_r, 2 * NT)
            norm_stats(s_r, s_bn, s_ve)
            dve.wait_ge(s_wrs, 1)
            v.tensor_tensor(w_lo[:, WR_AT:3 * GW], wr_raw.rearrange("p k c -> p (k c)"),
                            w_hi[:, WR_AT:3 * GW].bitcast(F32), ALU.subtract).then_inc(s_wrs, 1)
            dve.wait_ge(s_rs, 1)
            dve.wait_ge(s_lnw, 32)
            for t in range(NT):
                norm_apply(t, s_ln)
                if t:
                    turned_low(2 * t - 2, s_x1hi, s_x1lo)
                    turned_low(2 * t - 1, s_x1hi, s_x1lo)
            turned_low(2 * NT - 2, s_x1hi, s_x1lo)
            turned_low(2 * NT - 1, s_x1hi, s_x1lo)

            n = [0]

            def step(ins):
                n[0] += 1
                ins.then_inc(s_rt, 1)

            def settle():
                dve.wait_ge(s_rt, n[0])

            def wide(x, k):
                return x.unsqueeze(2).broadcast_to([P, NT, k])

            def top(out, o, k):
                eq = eq_g if k == GROUPS else eq_e
                step(v.tensor_reduce(col[0], o, AXX, ALU.max))
                settle()
                step(v.tensor_tensor(eq, o, wide(col[0], k), ALU.is_equal))
                settle()
                step(v.tensor_tensor(eq, eq, rank[:, 0:k].unsqueeze(1).broadcast_to([P, NT, k]), ALU.mult))
                settle()
                step(v.tensor_reduce(col[1], eq, AXX, ALU.max))
                settle()
                step(v.tensor_tensor(out, eq, wide(col[1], k), ALU.is_equal))
                settle()

            dve.wait_ge(s_rp, 1)
            dve.wait_ge(s_rb, 16)
            dve.wait_ge(s_rc, 7)
            step(v.tensor_tensor(logit, bank[4][:, 0:NT * 36].rearrange("p (t c) -> p t c", t=NT),
                                 r_bias.unsqueeze(1).broadcast_to([P, NT, 36]), ALU.add))
            settle()
            g_logit = logit[:, :, 0:GROUPS]
            top(one_g, g_logit, GROUPS)
            step(v.tensor_tensor(dif_g, g_logit, wide(col[0], GROUPS), ALU.subtract))
            assert n[0] == RT_GROUP, n
            step(v.tensor_tensor(picked, logit[:, :, GROUPS:36].rearrange("p t (g e) -> p t e g", g=GROUPS),
                                 one_g.unsqueeze(2).broadcast_to([P, NT, EG, GROUPS]), ALU.mult))
            settle()
            step(v.tensor_reduce(e_log, picked, AXX, ALU.add))
            settle()
            top(one_e[0], e_log, EG)
            step(v.tensor_copy(col[2], col[0]))
            step(v.scalar_tensor_tensor(out=e_log, in0=one_e[0], scalar=TAKEN, in1=e_log, op0=ALU.mult, op1=ALU.add))
            settle()
            top(one_e[1], e_log, EG)
            step(v.tensor_tensor(col[5], col[0], col[2], ALU.subtract))
            assert n[0] == RT_SECOND, n
            for k in range(2):
                step(v.tensor_tensor(one[k].rearrange("p t (g e) -> p t g e", g=GROUPS),
                                     one_g.unsqueeze(3).broadcast_to([P, NT, GROUPS, EG]),
                                     one_e[k].unsqueeze(2).broadcast_to([P, NT, GROUPS, EG]), ALU.mult))
            settle()
            v.tensor_tensor(chosen[:, :, :], one[0], one[1], ALU.add).then_inc(s_cho, 1)
            for k in range(2):
                step(v.tensor_tensor(tok[k], one[k], wide(token, NE), ALU.mult))
            step(v.tensor_scalar(twice, one[1], 2.0, None, ALU.mult))
            dve.wait_ge(s_ra, 2)
            step(v.tensor_reduce(col[6], dif_g, AXX, ALU.add))
            step(v.tensor_scalar(col[7], col[5], 1.0, None, ALU.add))
            settle()
            step(v.tensor_tensor(col[6], col[6], col[7], ALU.mult))
            settle()
            step(v.reciprocal(gate_w[0], col[6]))
            settle()
            step(v.tensor_tensor(gate_w[1], gate_w[0], col[5], ALU.mult))
            dve.wait_ge(s_pos, 1)
            v.tensor_reduce(most[:, :], bank[6][:, NT * NE:(NT + 1) * NE], AXX, ALU.max).then_inc(s_most, 1)
            for k in range(2):
                settle()
                step(v.tensor_tensor(place, one[k], bank[6][:, 0:NT * NE].rearrange("p (t e) -> p t e", t=NT),
                                     ALU.mult))
                settle()
                step(v.tensor_reduce(col[8 + k], place, AXX, ALU.add))
            settle()

            def tables(b):
                m = [TB * b]

                def tb(ins):
                    m[0] = m[0] + 1
                    ins.then_inc(s_tb, 1)

                def tb_settle():
                    dve.wait_ge(s_tb, m[0])

                for k in range(2):
                    tb(v.tensor_scalar(col[8 + k], col[8 + k], 0.0 if isinstance(b, int) else -float(P), None,
                                       ALU.add))
                tb_settle()
                for k in range(2):
                    tb(v.tensor_tensor(seat[k], count_c.unsqueeze(1).broadcast_to([P, NT, P]), wide(col[8 + k], P),
                                       ALU.is_equal))
                dve.wait_ge(s_tabp, b + 1)
                got, nth = bank[7][:, 0:NE], bank[7][:, NE:2 * NE]
                skip = place.rearrange("p t e -> p (t e)")[:, 0:NE]
                both = place.rearrange("p t e -> p (t e)")[:, NE:2 * NE]
                pick = place.rearrange("p t e -> p (t e)")[:, 2 * NE:3 * NE]
                tb(v.tensor_scalar(skip, nth, 0.0, skip_row, ALU.is_equal, ALU.mult))
                tb(v.tensor_scalar(both, nth, float(SEQ), -float(SEQ), ALU.mult, ALU.add))
                tb(v.tensor_copy(pick, got))
                tb_settle()
                tb(v.tensor_tensor(both, both, pick, ALU.add))
                tb(v.tensor_tensor(pick, pick, skip, ALU.add))
                tb_settle()
                v.tensor_copy(row_got[:, :], pick).then_inc(s_rows, 1)
                v.tensor_tensor(row_put[:, :], both, skip, ALU.add).then_inc(s_rows, 1)

            def split_expert(T, par, q):
                dve.wait_ge(s_ehi, 3 * T + q + 1)
                v.tensor_tensor(group(w_lo, ESLOT[q]),
                                raw[:, par * EW + q * GW:par * EW + (q + 1) * GW].rearrange("p (u c) -> p u c", u=4),
                                group(w_hi, ESLOT[q]).bitcast(F32), ALU.subtract).then_inc(s_elo, 1)

            def tokens_low(T, par, half):
                dve.wait_ge(s_xh, 2 * T + half + 1)
                v.tensor_tensor(xg(lo_flat, par)[:, 4 * half:4 * half + 4, :],
                                bank[2 + half][:, :].rearrange("p (k c) -> p k c", k=4),
                                xg(hi_flat, par)[:, 4 * half:4 * half + 4, :].bitcast(F32), ALU.subtract)\
                    .then_inc(s_xl, 1)


            def run(b, base):
                tables(b)
                for q in range(2):
                    split_expert(base, 0, q)
                for half in range(2):
                    tokens_low(base, 0, half)

                def expert(T, par, last):
                    dve.wait_ge(s_silu, T + 1)
                    v.tensor_tensor(h_buf, silu_g, bank[0][:, DE:2 * DE], ALU.mult).then_inc(s_h, 1)
                    if not last:
                        tokens_low(T + 1, 1 - par, 0)
                    dve.wait_ge(s_hh, T + 1)
                    v.tensor_tensor(ht(lo_flat), bank[1][:, 0:DE].rearrange("p (k c) -> p k c", k=2),
                                    ht(hi_flat).bitcast(F32), ALU.subtract).then_inc(s_hl, 1)
                    if not last:
                        tokens_low(T + 1, 1 - par, 1)
                        split_expert(T + 1, 1 - par, 0)
                        split_expert(T + 1, 1 - par, 1)
                    dve.wait_ge(s_used, 3 * T + 3)
                    wait_count(dve, s_put[par], arrived(T - 2, par))
                    v.tensor_copy(y_out[par][:, 512:1024], bank[5][:, :]).then_inc(s_outv, 1)

                for par in range(2):
                    expert(base + par, par, False)
                with dve.Fori(1, NE // 2 - 1) as i:
                    for par in range(2):
                        expert(base + 2 * i + par, par, False)
                for par in range(2):
                    expert(base + NE - 2 + par, par, par == 1)
                for par in range(2):
                    dve.wait_ge(s_put[par], 8 * (base + NE))

            expert_blocks(dve, run)

            for t in range(NT):
                dve.wait_ge(s_y0, t + 1)
                first, second = raw[:, t * 2 * DM:t * 2 * DM + DM], raw[:, t * 2 * DM + DM:(t + 1) * 2 * DM]
                v.scalar_tensor_tensor(out=second, in0=second, scalar=gate_w[1][:, t:t + 1], in1=first, op0=ALU.mult,
                                       op1=ALU.add).then_inc(s_r2, 1)
            for t in range(NT):
                dve.wait_ge(s_r2, t + 1)
                v.scalar_tensor_tensor(out=mine[:, t, :], in0=mine[:, t, :], scalar=ALPHA,
                                       in1=raw[:, t * 2 * DM + DM:(t + 1) * 2 * DM], op0=ALU.mult, op1=ALU.add)\
                    .then_inc(s_r2, 1)
            dve.wait_ge(s_r2, 2 * NT)
            norm_stats(s_r2, s_bn2, s_ve2)
            dve.wait_ge(s_rs2, 1)
            dve.wait_ge(s_lnw2, 32)
            for t in range(NT):
                norm_apply(t, s_ln2)
                if t:
                    turned_low(2 * t - 2, s_x2hi, s_x2lo)
                    turned_low(2 * t - 1, s_x2hi, s_x2lo)
            turned_low(2 * NT - 2, s_x2hi, s_x2lo)
            turned_low(2 * NT - 1, s_x2hi, s_x2lo)
            for u in range(2 * NT):
                half, t = u // NT, u % NT
                dve.wait_ge(s_sig, u + 1)
                o = raw[:, t * DM + half * 512:t * DM + (half + 1) * 512]
                v.tensor_tensor(o, o, ple[:, t, half * 512:(half + 1) * 512], ALU.mult).then_inc(s_mix, 1)
                dve.wait_ge(s_mix, 2 * u + 1)
                v.tensor_tensor(o, o, mine[:, t, half * 512:(half + 1) * 512], ALU.add).then_inc(s_mix, 1)

        @block.tensor
        def _(pe):
            t_ = nc.tensor

            def three(o, lh, ll, rh, rl, first, last):
                t_.matmul(o, lh, rh, start=first, stop=False)
                t_.matmul(o, lh, rl, start=False, stop=False)
                return t_.matmul(o, ll, rh, start=False, stop=last)

            def project(n):
                grp, j = kind(n)
                pe.wait_ge(s_wlo, n + 1)
                if n >= 2:
                    pe.wait_ge(s_evac, n - 1)
                o = proj_bank[n % 2]
                wh, wl = slot(w_hi, n), slot(w_lo, n)
                if grp is None or j in (0, 1, 3, 4):
                    for k in range(NK):
                        if n == 0 and k % 2 == 0:
                            pe.wait_ge(s_xlo, k // 2 + 1)
                        mm = three(o[:, :], wh[:, k, :], wl[:, k, :], a_hi[:, k, :], a_lo[:, k, :],
                                   k == 0, k == NK - 1)
                else:
                    for t in range(NT):
                        for k in range(NK):
                            mm = three(o[:, t * P:(t + 1) * P], a_hi[:, k, t * P:(t + 1) * P],
                                       a_lo[:, k, t * P:(t + 1) * P], wh[:, k, :], wl[:, k, :],
                                       k == 0, k == NK - 1)
                mm.then_inc(s_proj, 1)

            def gates_a():
                pe.wait_ge(s_w16s, 2)
                for t in range(NT):
                    for k in range(NK):
                        mm = three(lstm_bank[0][:, t * 16:(t + 1) * 16], a_hi[:, k, t * P:(t + 1) * P],
                                   a_lo[:, k, t * P:(t + 1) * P], w16_hi[:, k, :], w16_lo[:, k, :],
                                   k == 0, k == NK - 1)
                mm.then_inc(s_gate_p, 1)
                pe.wait_ge(s_setup, 16)
                pe.wait_ge(s_gate_e, 2)
                for t in range(NT):
                    t_.transpose(lstm_bank[1][0:HM, t * P:(t + 1) * P], if_pre[:, t, 0:4], ident[:, :])
                    mm = t_.transpose(turn_bank[0:HM, t * P:(t + 1) * P], if_pre[:, t, 4:8], ident[:, :])
                mm.then_inc(s_row_p, 1)

            def gates_b():
                pe.wait_ge(s_row_v, 10)
                for t in range(NT):
                    mm = t_.transpose(lstm_bank[0][:, t * HM:(t + 1) * HM], i_row[:, t * P:(t + 1) * P],
                                      ident[0:HM, 0:HM])
                mm.then_inc(s_col_p, 1)
                pe.wait_ge(s_row_a, 3)
                for t in range(NT):
                    mm = t_.transpose(lstm_bank[0][:, 16 + t * HM:16 + (t + 1) * HM], g_row[:, t * P:(t + 1) * P],
                                      ident[0:HM, 0:HM])
                mm.then_inc(s_col_p, 1)

            def index_scores():
                pe.wait_ge(s_evac, SMALL)
                for n in range(3 * HI_):
                    b, h = n // HI_ + 1, n % HI_
                    if n >= 2:
                        pe.wait_ge(s_relu, n - 1)
                    rows = slice(DI * (h % 4), DI * (h % 4 + 1))
                    t_.matmul(score_bank[n % 2][:, 0:(b + 1) * P], qi[rows, h // 4, b * P:(b + 1) * P],
                              ki[rows, 0:(b + 1) * P], start=True, stop=True).then_inc(s_idx, 1)

            def qk(g, u):
                U, hh, b = 8 * g + u, u // NT, u % NT
                if u == 0:
                    pe.wait_ge(s_evac, piece_no(g, 1) + 1)
                if U >= 2:
                    pe.wait_ge(s_masked, U - 1)
                else:
                    pe.wait_ge(s_relu, 3 * HI_)
                rows = slice(DA * hh, DA * (hh + 1))
                t_.matmul(score_bank[U % 2][:, 0:(b + 1) * P], q_t[rows, g % 2, b * P:(b + 1) * P],
                          k_t[rows, g % 2, 0:(b + 1) * P], start=True, stop=True).then_inc(s_qk, 1)

            def turn(g, u):
                U, b = 8 * g + u, u % NT
                pe.wait_ge(s_exp, U + 1)
                if U:
                    pe.wait_ge(s_probt, U)
                for s in range(b + 1):
                    mm = t_.transpose(turn_bank[:, s * P:(s + 1) * P], prob[:, U % 2, s * P:(s + 1) * P], ident[:, :])
                mm.then_inc(s_turn, 1)

            def pv(g, u):
                U, hh, b = 8 * g + u, u // NT, u % NT
                pe.wait_ge(s_probt, U + 1)
                if u == 0:
                    pe.wait_ge(s_evac, piece_no(g, 2) + 1)
                    if g:
                        pe.wait_ge(s_ya, g)
                o = attn_bank[:, (2 * b + hh) * DA:(2 * b + hh + 1) * DA]
                for s in range(b + 1):
                    mm = t_.matmul(o, prob_t[:, U % 2, s * P:(s + 1) * P], v_a[:, g % 2, s, hh * DA:(hh + 1) * DA],
                                   start=s == 0, stop=s == b)
                mm.then_inc(s_pv, 1)

            def lstm_broadcast(h):
                if h:
                    pe.wait_ge(s_hid, 2 * h)
                else:
                    pe.wait_ge(s_col_v, 2)
                t_.matmul(lstm_bank[1][:, :], sel_head[:, h, :], nega_row, start=True, stop=True).then_inc(s_gbc, 1)

            def lstm_qk(h, b):
                if b == 0:
                    pe.wait_ge(s_conv, 2 * (h + 1))
                    if h:
                        pe.wait_ge(s_hid, 2 * h)
                elif b == 1:
                    pe.wait_ge(s_gadd, 4 * (h + 1))
                else:
                    pe.wait_ge(s_mw, 4 * h + b - 1)
                t_.matmul(lstm_bank[b % 2][:, 0:SEQ - b * P], qk_m[:, 1, b * P:(b + 1) * P], qk_m[:, 0, b * P:SEQ],
                          start=True, stop=True).then_inc(s_mqk, 1)

            def lstm_num(h):
                pe.wait_ge(s_mw, 4 * (h + 1))
                pe.wait_ge(s_evac, piece_no(h, 5) + 1)
                for t in range(NT):
                    o = lstm_bank[t // 2][:, (t % 2) * 129:(t % 2 + 1) * 129]
                    for s in range(t + 1):
                        mm = t_.matmul(o, weight[:, LO_[s] + (t - s) * P:LO_[s] + (t - s + 1) * P],
                                       v_m[:, h % 2, s, :], start=s == 0, stop=s == t)
                mm.then_inc(s_mnum, 1)

            def slot_work(g, j):
                if j == 0:
                    lstm_broadcast(g)
                for e in range(2):
                    if j < 4:
                        qk(g, 2 * j + e)
                    if 1 <= j <= 4:
                        turn(g, 2 * j - 2 + e)
                    if 2 <= j <= 5:
                        pv(g, 2 * j - 4 + e)
                if 1 <= j <= 4:
                    lstm_qk(g, j - 1)
                if j == 5:
                    lstm_num(g)

            for n in range(SMALL):
                project(n)
                if n == 1:
                    gates_a()
            gates_b()
            index_scores()
            for g in range(NG):
                for j in range(PIECES):
                    project(piece_no(g, j))
                    if g:
                        slot_work(g - 1, j)
            for j in range(PIECES):
                slot_work(NG - 1, j)

            pe.wait_ge(s_ya, NG)
            pe.wait_ge(s_ym, NG)
            for k in range(NK):
                if k >= 4:
                    pe.wait_ge(s_ylo, k - 3)
                for t in range(NT):
                    mm = t_.transpose(bank[k % 4][:, t * P:(t + 1) * P], y[:, t, k * P:(k + 1) * P], ident[:, :])
                mm.then_inc(s_yt, 1)
            pe.wait_ge(s_ylo, NK)

            def token_major(q, o, weights):
                wh, wl = group(w_hi, OSLOT[q]), group(w_lo, OSLOT[q])
                for kk in range(4):
                    k = 4 * (q % 2) + kk
                    for t in range(NT):
                        mm = three(o[t][:, :], a_hi[:, k, t * P:(t + 1) * P], a_lo[:, k, t * P:(t + 1) * P],
                                   wh[:, kk, :], wl[:, kk, :], k == 0, k == NK - 1)
                mm.then_inc(weights, 1)

            for q in range(4):
                pe.wait_ge(s_olo, q + 1)
                token_major(q, bank[4:8] if q < 2 else bank[0:4], s_wo)

            def turn_tile(t, done, low):
                for half in range(2):
                    u = 2 * t + half
                    if u >= 4:
                        pe.wait_ge(low, u - 3)
                    for k in range(4):
                        mm = t_.transpose(bank[u % 4][:, k * P:(k + 1) * P],
                                          mine[:, t, (4 * half + k) * P:(4 * half + k + 1) * P], ident[:, :])
                    mm.then_inc(done, 1)

            wr_hi = w_hi[:, WR_AT:3 * GW].rearrange("p (k c) -> p k c", k=NK)
            wr_lo = w_lo[:, WR_AT:3 * GW].rearrange("p (k c) -> p k c", k=NK)

            def route(t):
                pe.wait_ge(s_x1lo, 2 * t + 2)
                for k in range(NK):
                    mm = three(bank[4][:, t * 36:(t + 1) * 36], a_hi[:, k, t * P:(t + 1) * P],
                               a_lo[:, k, t * P:(t + 1) * P], wr_hi[:, k, :], wr_lo[:, k, :], k == 0, k == NK - 1)
                if t == NT - 1:
                    mm.then_inc(s_rp, 1)

            for t in range(NT):
                pe.wait_ge(s_ln, 2 * t + 2)
                turn_tile(t, s_x1t, s_x1lo)
                if t == 1:
                    pe.wait_ge(s_wrs, 2)
                if t:
                    route(t - 1)
            route(NT - 1)

            pe.wait_ge(s_plo, 2)
            for u in range(2 * NT):
                t, half = u // 2, u % 2
                if u >= 4:
                    pe.wait_ge(s_pev, u - 3)
                for k in range(2):
                    mm = three(bank[u % 4][:, :], a_hi[:, k, t * P:(t + 1) * P], a_lo[:, k, t * P:(t + 1) * P],
                               group(w_hi, 0)[:, 2 * half + k, :], group(w_lo, 0)[:, 2 * half + k, :],
                               k == 0, k == 1)
                mm.then_inc(s_pp, 1)

            pe.wait_ge(s_cho, 1)
            pe.wait_ge(s_rc, 7)
            for t in range(NT):
                for s in range(t + 1):
                    t_.matmul(bank[6][:, t * NE:(t + 1) * NE], tri[:, :] if s == t else ones[:, :], chosen[:, s, :],
                              start=s == 0, stop=s == t)
            for s in range(NT):
                mm = t_.matmul(bank[6][:, NT * NE:(NT + 1) * NE], ones[:, :], chosen[:, s, :], start=s == 0,
                               stop=s == NT - 1)
            mm.then_inc(s_pos, 1)
            pe.wait_ge(s_pev, 2 * NT)

            def tables(b):
                pe.wait_ge(s_tb, TB_SEATS + TB * b)
                for part, cols in enumerate((tok, (one[0], twice))):
                    for k in range(2):
                        for t in range(NT):
                            mm = t_.matmul(bank[7][:, part * NE:(part + 1) * NE], seat[k][:, t, :], cols[k][:, t, :],
                                           start=k == 0 and t == 0, stop=k == 1 and t == NT - 1)
                mm.then_inc(s_tabp, 1)

            def turn_tokens(T, par, half, first=False):
                if half == 0:
                    pe.wait_ge(s_got[par], arrived(T, par))
                if not first:
                    pe.wait_ge(s_xl, 2 * T - 1 + half)
                for k in range(4):
                    mm = t_.transpose(bank[2 + half][:, k * P:(k + 1) * P],
                                      x_got[par][:, (4 * half + k) * P:(4 * half + k + 1) * P], ident[:, :])
                mm.then_inc(s_xt, 1)

            def run(b, base):
                tables(b)
                for half in range(2):
                    turn_tokens(base, 0, half, isinstance(b, int))

                def expert(T, par, last):
                    pe.wait_ge(s_xl, 2 * T + 2)
                    for q in range(2):
                        pe.wait_ge(s_elo, 2 * T + q + 1)
                        for kk in range(4):
                            k = 4 * q + kk
                            mm = three(bank[0][:, :], xg(hi_flat, par)[:, k, :], xg(lo_flat, par)[:, k, :],
                                       group(w_hi, ESLOT[q])[:, kk, :], group(w_lo, ESLOT[q])[:, kk, :],
                                       k == 0, k == NK - 1)
                        mm.then_inc(s_used, 1)
                    if not last:
                        turn_tokens(T + 1, 1 - par, 0)
                    pe.wait_ge(s_h, T + 1)
                    for k in range(2):
                        mm = t_.transpose(bank[1][:, k * P:(k + 1) * P], h_buf[:, k * P:(k + 1) * P], ident[:, :])
                    mm.then_inc(s_th, 1)
                    if not last:
                        turn_tokens(T + 1, 1 - par, 1)
                    pe.wait_ge(s_hl, T + 1)
                    pe.wait_ge(s_elo2, T + 1)
                    wait_count(pe, s_outa, T)
                    wait_count(pe, s_outv, T)
                    for half in range(2):
                        for k in range(2):
                            u = 2 * half + k
                            mm = three(bank[4 + half][:, :], ht(hi_flat)[:, k, :], ht(lo_flat)[:, k, :],
                                       group(w_hi, ESLOT[2])[:, u, :], group(w_lo, ESLOT[2])[:, u, :],
                                       k == 0, k == 1)
                    mm.then_inc(s_used, 1)

                for par in range(2):
                    expert(base + par, par, False)
                with pe.Fori(1, NE // 2 - 1) as i:
                    for par in range(2):
                        expert(base + 2 * i + par, par, False)
                for par in range(2):
                    expert(base + NE - 2 + par, par, par == 1)
                for par in range(2):
                    pe.wait_ge(s_put[par], 8 * (base + NE))

            pe.wait_ge(s_most, 1)
            expert_blocks(pe, run)

            for t in range(NT):
                pe.wait_ge(s_ln2, 2 * t + 2)
                turn_tile(t, s_x2t, s_x2lo)
            pe.wait_ge(s_x2lo, 2 * NT)
            for q in range(4):
                pe.wait_ge(s_glo, q + 1)
                token_major(q, bank[4:8] if q < 2 else bank[0:4], s_gp)


def layout(x, p, w_in, b_igate, b_fgate, conv_w, conv_b, gn_w, w_out, ln1_g, ln1_b, router_group_w, router_group_b,
           router_expert_w, router_expert_b, expert_w_gate, expert_w_up, expert_w_down, ln2_g, ln2_b, ple_gate_w,
           ple_proj_w):
    import numpy as np

    def rows(w):
        return w.reshape(w.shape[0] // P, P, w.shape[1]).transpose(1, 0, 2)

    def halves(w, parts):
        k = w.shape[0] // P
        w = w.reshape(parts, k // parts, P, 2, 512).transpose(3, 0, 2, 1, 4)
        return w.reshape(2 * parts, P, k // parts * 512)

    def experts(gate, up, down):
        gu = np.stack([w.reshape(NE, NK, P, DE) for w in (gate, up)], axis=3).transpose(0, 2, 1, 3, 4)
        dn = down.reshape(NE, 2, P, 2, 512).transpose(0, 2, 3, 1, 4)
        return np.concatenate([gu.reshape(NE, P, 2 * GW), dn.reshape(NE, P, GW)], axis=2)

    wi = np.asarray(w_in)[0]
    at = np.cumsum([0, 512, 512, 512, 256, 32, 8, 512, 512, 512, 512, 4, 4])
    qa, ka, va, qi, ki, wx, qm, km, vm, om, im, fm = (wi[:, at[i]:at[i + 1]] for i in range(12))
    pieces = [qi[:, 0:P], qi[:, P:2 * P], np.concatenate([ki] * 4, axis=1)]
    for g in range(NG):
        pieces += [m[:, g * P:(g + 1) * P] for m in (qa, ka, va, qm, km, vm, om)]
    cw, cb = np.asarray(conv_w)[0], np.asarray(conv_b)[0]
    return {
        "xT": rows(np.asarray(x)[0].T),
        "w_in": np.stack([rows(w).reshape(P, PW) for w in pieces]),
        "w16": rows(np.concatenate([wx, im, fm], axis=1)),
        "if_bias": np.concatenate([np.asarray(b_igate)[0], np.asarray(b_fgate)[0]]),
        "conv_wb": np.concatenate([cw, cb[None]]).reshape(5, 2 * HM, P).transpose(2, 1, 0),
        "gn_w": np.asarray(gn_w)[0],
        "x": np.asarray(x)[0],
        "pT": rows(np.asarray(p)[0, 0].T),
        "w_out": halves(np.asarray(w_out)[0], 2),
        "ple_gate": halves(np.asarray(ple_gate_w)[0], 2),
        "ple_proj": halves(np.asarray(ple_proj_w)[0], 1).transpose(1, 0, 2).reshape(P, GW),
        "ln1_g": np.asarray(ln1_g)[0], "ln1_b": np.asarray(ln1_b)[0],
        "ln2_g": np.asarray(ln2_g)[0], "ln2_b": np.asarray(ln2_b)[0],
        "w_router": rows(np.concatenate([np.asarray(router_group_w)[0], np.asarray(router_expert_w)[0]], axis=1)),
        "r_bias": np.concatenate([np.asarray(router_group_b)[0], np.asarray(router_expert_b)[0]]),
        "w_exp": experts(*(np.asarray(w)[0] for w in (expert_w_gate, expert_w_up, expert_w_down))),
    }


def kernel(**inputs):
    import numpy as _np
    import concourse.bacc as _bacc
    from concourse import mybir as _mybir
    from concourse.bass_utils import run_bass_kernel_spmd as _run

    nc = _bacc.Bacc("TRN2", target_bir_lowering=False, num_devices=1)
    arrays, views = {}, {}
    for name, a in layout(**inputs).items():
        a = _np.ascontiguousarray(a)
        arrays[f"in_{name}_dram"] = a
        views[name] = nc.dram_tensor(f"in_{name}_dram", a.shape, _mybir.dt.from_np(a.dtype), kind="ExternalInput").ap()
    out = nc.dram_tensor("out_dram", (SEQ, DM), _mybir.dt.float32, kind="ExternalOutput").ap()
    x1 = nc.dram_tensor("x1_dram", (SEQ, DM), _mybir.dt.float32, kind="Internal").ap()
    pairs = nc.dram_tensor("pair_dram", (2 * SEQ, DM), _mybir.dt.float32, kind="Internal").ap()
    hybrid_layer(nc, views, out, x1, pairs)
    r = _run(nc, [arrays], core_ids=[0])
    return r.results[0]["out_dram"].reshape(1, SEQ, DM)
```

```python
import concourse.bass as bass
from concourse import mybir
from contextlib import ExitStack

F32 = mybir.dt.float32
F32R = mybir.dt.float32r
BF16 = mybir.dt.bfloat16
I32 = mybir.dt.int32
ALU = mybir.AluOpType
ACT = mybir.ActivationFunctionType
AXX = mybir.AxisListType.X

P = 128
SEQ, DM = 512, 1024
NT, NK = SEQ // P, DM // P
HA, DA = 8, 64
HI_, DI = 8, 32
HM = 4
TOPK = min(256, SEQ // 4)
ALPHA = 2.0 ** 0.25
EPS = 1e-5
NG = 4
TALL = 4
STEPS = TALL + NT
SMALL = 3
NPIECE = SMALL + NG * TALL
NSTEP = SMALL + NG * STEPS
RING = 3
PW = NK * P
WIDE = 3 * P
NE, EG, GROUPS = 32, 8, 4
DE = 256
BLOCKS = SEQ // P
GW = 2048
SKIP = 4096
BIG = 1.0e30
TAKEN = -3.0e38


def hybrid_layer(nc, d, out, x1_dram, pair_dram):
    ctx = ExitStack()
    with ctx:
        def sb(name, shape, dt=F32):
            return ctx.enter_context(nc.sbuf_tensor(name, shape, dt))

        def sem(name):
            return ctx.enter_context(nc.semaphore(name))

        raw = sb("raw", [P, 12 * PW])
        w_hi = sb("w_hi", [P, 6 * PW], F32R)
        w_lo = sb("w_lo", [P, 6 * PW], F32R)
        a_hi = sb("a_hi", [P, NK, SEQ], F32R)
        a_lo = sb("a_lo", [P, NK, SEQ], F32R)
        res = sb("res", [P, NT * DM])
        y = sb("y", [P, NT, DM])
        pa = sb("pa", [P, 9536])

        ident = sb("ident", [P, P])
        sel_head = sb("sel_head", [HM, HM, P])
        dist = sb("dist", [P, SEQ])
        q_scale = sb("q_scale", [P, NG])
        conv_wb = sb("conv_wb", [P, 2 * HM, 5])
        gn_half = sb("gn_half", [P, HM * P])
        if_bias = sb("if_bias", [P, 8])
        w16_hi = sb("w16_hi", [P, NK, 16], F32R)
        w16_lo = sb("w16_lo", [P, NK, 16], F32R)
        w_head = sb("w_head", [P, NT, HI_])
        if_pre = sb("if_pre", [P, NT, 8])
        a_col = sb("a_col", [P, NT, HM])
        em_col = sb("em_col", [P, NT, HM])
        small = sb("small", [P, 160])
        tri = sb("tri", [P, P], BF16)
        ones = sb("ones", [P, P], BF16)
        chosen = sb("chosen", [P, NT, NE], BF16)
        row_got, row_put = sb("row_got", [P, NE], I32), sb("row_put", [P, NE], I32)
        at_got, at_put = sb("at_got", [P, 2], I32), sb("at_put", [P, 2], I32)
        most = sb("most", [P, 1], I32)

        bank = [ctx.enter_context(nc.psum_tensor(f"bank{i}", [P, 512], F32)) for i in range(8)]
        proj_bank = bank[0:2]
        score_bank = bank[2:4]
        turn_bank, attn_bank = bank[4], bank[5]
        lstm_bank = bank[6:8]
        turned_1 = [bank[5], bank[6], bank[7], bank[2]]
        turned_2 = bank[0:4]
        gu_bank = [bank[0], bank[6]]
        index_bank = [bank[2], bank[3], bank[5], bank[7]]

        x_raw = res[:, :].rearrange("p (k t) -> p k t", k=NK)
        RAWS = 2
        wide_raw = raw[:, RAWS * PW:RAWS * PW + NK * WIDE]
        scratch = raw[:, RAWS * PW + NK * WIDE:12 * PW]
        index_hi, index_lo = (m[:, 3 * PW:3 * PW + SMALL * SEQ].rearrange("p (a t) -> p a t", a=SMALL)
                              for m in (w_hi, w_lo))
        relu = scratch[:, 1536:2560].rearrange("p (a s) -> p a s", a=2)
        SO = [None, 0, 256, 640]
        score = scratch[:, 2560:3712]
        left = scratch[:, 3712:4864]
        i_row = scratch[0:HM, 4864:5376]
        f_row = scratch[0:HM, 5376:5888]
        c_row = scratch[0:HM, 5888:6400]
        g_row = scratch[0:HM, 6400:6912]
        w16 = scratch[:, 6912:7040].rearrange("p (k c) -> p k c", k=NK)
        masked = scratch[:, 0:1024].rearrange("p (a s) -> p a s", a=2)
        prob = scratch[:, 1024:2048].rearrange("p (a s) -> p a s", a=2)
        prob_t = scratch[:, 2048:3072].rearrange("p (a s) -> p a s", a=2)
        LO_ = [0, 512, 896, 1152, 1280]
        decay = res[:, 0:1280]
        weight = res[:, 1280:2560]
        conv = res[:, 2560:3584].rearrange("p (a t) -> p a t", a=2)
        tanh_c = res[:, 3584:4096]

        at = [0]

        def take(n):
            at[0] += n
            return pa[:, at[0] - n:at[0]]

        q_t = take(1024).rearrange("p (a t) -> p a t", a=2)
        k_t = take(1024).rearrange("p (a t) -> p a t", a=2)
        v_a = take(1024).rearrange("p (a s c) -> p a s c", a=2, s=NT)
        mdist = take(1280)
        MO = [0, 128, 384, 768]
        pre = take(2 * 516).rearrange("p (a t) -> p a t", a=2)
        qk_m = take(1024).rearrange("p (a t) -> p a t", a=2)
        v_m = take(2 * NT * 129).rearrange("p (a s c) -> p a s c", a=2, s=NT)
        o_m = take(1024).rearrange("p (a s c) -> p a s c", a=2, s=NT)
        hidden = take(NT * 129).rearrange("p (s c) -> p s c", s=NT)
        nega_row = take(512)[0:HM, :]
        assert at[0] <= 9536, at

        row_max = small[:, 0:2]
        neg_max = small[:, 2:4]
        row_sum = small[:, 8:16].rearrange("p (t h) -> p t h", h=2)
        row_inv = small[:, 16:24].rearrange("p (t h) -> p t h", h=2)
        best = small[:, 24:48].rearrange("p (b n) -> p b n", b=3)
        den = small[:, 48:52]
        den_inv = small[:, 52:56]
        stats = small[:, 56:80].rearrange("p (s c) -> p s c", s=NT)
        mean_var = small[:, 80:88].rearrange("p (s c) -> p s c", s=NT)
        rstd = small[:, 88:92]
        minus_half = small[:, 92:96]

        ple = pa[:, 0:4096].rearrange("p (t c) -> p t c", t=NT)
        ln_g, ln_b = pa[:, 4096:5120], pa[:, 5120:6144]
        at[0] = 6144
        logit = take(NT * 36).rearrange("p (t c) -> p t c", t=NT)
        r_bias = take(36)
        one_g, eq_g, dif_g = [take(NT * GROUPS).rearrange("p (t g) -> p t g", t=NT) for _ in range(3)]
        one_e = [take(NT * EG).rearrange("p (t e) -> p t e", t=NT) for _ in range(2)]
        e_log, eq_e = [take(NT * EG).rearrange("p (t e) -> p t e", t=NT) for _ in range(2)]
        picked = take(NT * NE).rearrange("p (t e g) -> p t e g", t=NT, e=EG)
        col = [take(NT) for _ in range(16)]
        one = [take(NT * NE).rearrange("p (t e) -> p t e", t=NT) for _ in range(2)]
        tok = [take(NT * NE).rearrange("p (t e) -> p t e", t=NT) for _ in range(2)]
        twice = take(NT * NE).rearrange("p (t e) -> p t e", t=NT)
        place = take(NT * NE).rearrange("p (t e) -> p t e", t=NT)
        seat = [take(NT * P).rearrange("p (t c) -> p t c", t=NT) for _ in range(2)]
        count_c = take(P)
        rank = take(EG)
        token = take(NT)
        skip_row = take(1)
        silu_g = take(DE)
        h_buf = take(DE)
        assert at[0] <= 9536, at
        y_flat = y[:, :, :].rearrange("p t c -> p (t c)")
        x_got = [y_flat[:, i * DM:(i + 1) * DM] for i in range(2)]
        y_out = [y_flat[:, (2 + i) * DM:(3 + i) * DM] for i in range(2)]
        hi_flat = a_hi[:, :, :].rearrange("p k t -> p (k t)")
        lo_flat = a_lo[:, :, :].rearrange("p k t -> p (k t)")

        def xg(m, par):
            return m[:, par * DM:(par + 1) * DM].rearrange("p (k c) -> p k c", k=NK)

        def pair_of(t):
            return raw[:, 2 * GW + t * 2 * DM:2 * GW + (t + 1) * 2 * DM].rearrange("p (k c) -> p k c", k=2)

        def ht(m):
            return m[:, 2 * DM:2 * DM + DE].rearrange("p (k c) -> p k c", k=2)

        wr_raw = y_flat[:, GW + 1024:GW + 1024 + NK * 36].rearrange("p (k c) -> p k c", k=NK)
        stat8 = small[:, 0:48].rearrange("p (t c) -> p t c", t=NT)
        mv8 = small[:, 48:56].rearrange("p (t c) -> p t c", t=NT)
        rs8 = small[:, 56:60]
        ve8 = small[:, 60:64]
        gate_w = [small[:, 64:68], small[:, 68:72]]
        proj_raw = pa[:, 0:GW]
        p_raw = pa[:, GW:GW + 1024].rearrange("p (k t) -> p k t", k=2)
        WR_AT = 3 * GW - NK * 36

        s_x = [sem(f"s_x{c}") for c in range(4)]
        s_const = sem("s_const")
        s_w16 = sem("s_w16")
        s_raw = [sem(f"s_raw{i}") for i in range(RAWS)]
        s_xhi, s_xlo = sem("s_xhi"), sem("s_xlo")
        s_w16s = sem("s_w16s")
        s_whi, s_wlo = sem("s_whi"), sem("s_wlo")
        s_wide, s_widehi, s_widelo = sem("s_wide"), sem("s_widehi"), sem("s_widelo")
        s_proj, s_evac = sem("s_proj"), sem("s_evac")
        s_setup = sem("s_setup")
        s_gate_p, s_gate_e = sem("s_gate_p"), sem("s_gate_e")
        s_row_p, s_row_v, s_row_a = sem("s_row_p"), sem("s_row_v"), sem("s_row_a")
        s_col_p, s_col_v = sem("s_col_p"), sem("s_col_v")
        s_ilo = sem("s_ilo")
        s_idx, s_relu, s_acc = sem("s_idx"), sem("s_relu"), sem("s_acc")
        s_fut = sem("s_fut")
        s_top, s_mdist, s_md0 = sem("s_top"), sem("s_mdist"), sem("s_md0")
        s_qk, s_masked, s_negmax, s_exp = sem("s_qk"), sem("s_masked"), sem("s_negmax"), sem("s_exp")
        s_turn, s_probt, s_pv = sem("s_turn"), sem("s_probt"), sem("s_pv")
        s_yinv, s_ya = sem("s_yinv"), sem("s_ya")
        s_gbc, s_gadd, s_dexp, s_dmask = sem("s_gbc"), sem("s_gadd"), sem("s_dexp"), sem("s_dmask")
        s_mqk, s_mw, s_mnum, s_hid = sem("s_mqk"), sem("s_mw"), sem("s_mnum"), sem("s_hid")
        s_cacc, s_ctanh, s_conv = sem("s_cacc"), sem("s_ctanh"), sem("s_conv")
        s_post, s_var, s_pow, s_ym = sem("s_post"), sem("s_var"), sem("s_pow"), sem("s_ym")
        s_idle = sem("s_idle")
        s_or = [sem(f"s_or{q}") for q in range(4)]
        s_ohi, s_olo, s_wo = sem("s_ohi"), sem("s_olo"), sem("s_wo")
        s_wot = sem("s_wot")
        s_yt, s_yhi, s_ylo = sem("s_yt"), sem("s_yhi"), sem("s_ylo")
        s_xn = [sem(f"s_xn{t}") for t in range(NT)]
        s_lnw, s_lnw2 = sem("s_lnw"), sem("s_lnw2")
        s_r, s_bn, s_ve, s_rs, s_ln = sem("s_r"), sem("s_bn"), sem("s_ve"), sem("s_rs"), sem("s_ln")
        s_x1d = sem("s_x1d")
        s_x1t, s_x1hi, s_x1lo = sem("s_x1t"), sem("s_x1hi"), sem("s_x1lo")
        s_rc = sem("s_rc")
        s_wr, s_wrs, s_rp, s_rt, s_ra = sem("s_wr"), sem("s_wrs"), sem("s_rp"), sem("s_rt"), sem("s_ra")
        s_rb = sem("s_rb")
        s_cho, s_pos, s_most = sem("s_cho"), sem("s_pos"), sem("s_most")
        s_tb, s_tabp, s_rows = sem("s_tb"), sem("s_tabp"), sem("s_rows")
        s_pr = sem("s_pr")
        s_pw, s_phi, s_plo, s_pp, s_pev = sem("s_pw"), sem("s_phi"), sem("s_plo"), sem("s_pp"), sem("s_pev")
        s_ew = [[sem(f"s_ew{a}{q}") for q in range(3)] for a in range(2)]
        s_ehi, s_elo, s_ehi2, s_elo2 = sem("s_ehi"), sem("s_elo"), sem("s_ehi2"), sem("s_elo2")
        s_gu, s_dn = sem("s_gu"), sem("s_dn")
        s_got = [sem(f"s_got{a}") for a in range(2)]
        s_put = [sem(f"s_put{a}") for a in range(2)]
        s_cg, s_cp = sem("s_cg"), sem("s_cp")
        s_xt, s_xh, s_xl = sem("s_xt"), sem("s_xh"), sem("s_xl")
        s_silu, s_h, s_th, s_hh, s_hl = sem("s_silu"), sem("s_h"), sem("s_th"), sem("s_hh"), sem("s_hl")
        s_outa, s_outv = sem("s_outa"), sem("s_outv")
        s_gw = [sem(f"s_gw{q}") for q in range(4)]
        s_pair = [sem(f"s_pair{t}") for t in range(NT)]
        s_ghi, s_glo, s_glo3, s_gt = sem("s_ghi"), sem("s_glo"), sem("s_glo3"), sem("s_gt")
        s_landed = sem("s_landed")
        s_r2, s_bn2, s_ve2, s_rs2, s_ln2 = [sem(n) for n in ("s_r2", "s_bn2", "s_ve2", "s_rs2", "s_ln2")]
        s_x2t, s_x2hi, s_x2lo = sem("s_x2t"), sem("s_x2hi"), sem("s_x2lo")
        s_sig, s_mix, s_out = sem("s_sig"), sem("s_mix"), sem("s_out")

        def kind(n):
            return (None, n) if n < SMALL else ((n - SMALL) // STEPS, (n - SMALL) % STEPS)

        def step_no(g, j):
            return SMALL + g * STEPS + j

        def step_of(i):
            return i if i < SMALL else step_no((i - SMALL) // TALL, (i - SMALL) % TALL)

        def piece_at(n):
            grp, j = kind(n)
            return n if grp is None else SMALL + TALL * grp + j if j < TALL else None

        def ring(m, i):
            return m[:, (i % RING) * PW:(i % RING + 1) * PW]

        def wide(m):
            return m[:, RING * PW:6 * PW]

        GATE_E = 3
        RT_GROUP, RT_SECOND = 7, 22
        TB, TB_SEATS = 9, 4
        def group(m, q):
            return m[:, q * GW:(q + 1) * GW].rearrange("p (u c) -> p u c", u=4)

        OSLOT = [1, 2, 0, 1]
        ESLOT = [1, 0, 2]
        ORAW = [0, GW, 8192, 8192 + GW]
        EW = 3 * GW
        mine = res[:, :].rearrange("p (t c) -> p t c", t=NT)

        def expert_blocks(eng, run):
            run(0, 0)
            fullest = eng.value_load(most[0:1, 0:1], min_val=0, max_val=SEQ)
            with eng.If(fullest > P):
                with eng.Fori(1, BLOCKS) as b:
                    run(b, b * NE)

        def wait_count(eng, sem_, value):
            if isinstance(value, int) and value <= 0:
                return
            eng.wait_ge(sem_, value)
            if not isinstance(value, int) and eng in (nc.sync, nc.gpsimd):
                eng.sem_inc(s_idle, 1)

        def arrived(T, par):
            return 8 * (T - par) + 16

        block = ctx.enter_context(nc.Block())

        @block.sync
        def _(sp):
            for c in range(4):
                sp.dma_start(x_raw[:, 2 * c:2 * c + 2, :], d["xT"][:, 2 * c:2 * c + 2, :]).then_inc(s_x[c], 16)
                if c == 0:
                    sp.dma_start(raw[:, 0:PW], d["w_in"][0, :, :]).then_inc(s_raw[0], 16)
            sp.dma_start(w16[:, :, :], d["w16"]).then_inc(s_w16, 16)
            sp.dma_start(if_bias[:, :], d["if_bias"].partition_broadcast(P)).then_inc(s_const, 16)
            sp.dma_start(conv_wb[:, :, :], d["conv_wb"]).then_inc(s_const, 16)
            sp.dma_start(gn_half[:, :], d["gn_w"].partition_broadcast(P)).then_inc(s_const, 16)
            for i in range(1, NPIECE):
                if i >= RAWS:
                    sp.wait_ge(s_wlo, i - RAWS + 1)
                r = i % RAWS
                sp.dma_start(raw[:, r * PW:(r + 1) * PW], d["w_in"][i, :, :]).then_inc(s_raw[r], 16)
                grp = (i - SMALL) // TALL
                if i >= SMALL and (i - SMALL) % TALL == (2 if grp else 0):
                    if grp:
                        sp.wait_ge(s_widelo, grp)
                    sp.dma_start(wide_raw, d["w_wide"][grp, :, :]).then_inc(s_wide, 16)
            sp.wait_ge(s_wlo, NPIECE)
            sp.wait_ge(s_widelo, NG)
            sp.wait_ge(s_mdist, 6)
            sp.wait_ge(s_col_v, 2)
            for q in range(4):
                sp.dma_start(raw[:, ORAW[q]:ORAW[q] + GW], d["w_out"][q, :, :]).then_inc(s_or[q], 16)
            sp.wait_ge(s_ya, NG)
            sp.wait_ge(s_ym, NG)
            for t in range(NT):
                sp.dma_start(mine[:, t, :], d["x"][t * P:(t + 1) * P, :]).then_inc(s_xn[t], 16)
            sp.dma_start(ln_g, d["ln1_g"].partition_broadcast(P)).then_inc(s_lnw, 16)
            sp.dma_start(ln_b, d["ln1_b"].partition_broadcast(P)).then_inc(s_lnw, 16)
            sp.dma_start(r_bias, d["r_bias"].partition_broadcast(P)).then_inc(s_rb, 16)
            sp.wait_ge(s_yt, NK)
            sp.dma_start(wr_raw, d["w_router"]).then_inc(s_wr, 16)

            def load(T, e, par, q):
                src = d["w_exp"][bass.ds(e, 1), :, q * GW:(q + 1) * GW].rearrange("a p c -> p (a c)")
                sp.dma_start(raw[:, par * EW + q * GW:par * EW + (q + 1) * GW], src).then_inc(s_ew[par][q], 16)

            def run(b, base):
                def ahead(e, par):
                    for q in range(2):
                        wait_count(sp, s_elo, 2 * (base + e) + q + 1)
                        load(base + e + 2, e + 2, par, q)
                    wait_count(sp, s_elo2, base + e)
                    load(base + e + 1, e + 1, 1 - par, 2)

                if isinstance(b, int):
                    sp.wait_ge(s_olo, 2)
                    for q in range(3):
                        load(0, 0, 0, q)
                    for q in range(3):
                        if q:
                            sp.wait_ge(s_olo, 2 + q)
                        load(1, 1, 1, q)
                    for t in range(NT):
                        sp.wait_ge(s_ln, 2 * t + 2)
                        sp.dma_start(x1_dram[t * P:(t + 1) * P, :], mine[:, t, :]).then_inc(s_x1d, 16)
                    sp.dma_start(ln_g, d["ln2_g"].partition_broadcast(P)).then_inc(s_lnw2, 16)
                    sp.dma_start(ln_b, d["ln2_b"].partition_broadcast(P)).then_inc(s_lnw2, 16)
                    sp.dma_start(p_raw, d["pT"]).then_inc(s_pr, 16)
                    sp.dma_start(proj_raw, d["ple_proj"]).then_inc(s_pw, 16)
                    for q in (0, 1, 2):
                        sp.wait_ge(*((s_elo2, 1) if q == 2 else (s_elo, q + 1)))
                        load(2, 2, 0, q)
                    for q in range(2):
                        sp.wait_ge(s_elo, q + 3)
                        load(3, 3, 1, q)
                else:
                    wait_count(sp, s_elo, 2 * base)
                    wait_count(sp, s_elo2, base)
                    for par in range(2):
                        for q in range(3 - par):
                            load(base + par, par, par, q)
                    ahead(0, 0)
                    ahead(1, 1)
                with sp.Fori(1, NE // 2 - 1) as i:
                    for par in range(2):
                        ahead(2 * i + par, par)
                wait_count(sp, s_elo2, base + NE - 2)
                load(base + NE - 1, NE - 1, 1, 2)
                wait_count(sp, s_elo, 2 * (base + NE))
                wait_count(sp, s_elo2, base + NE)

            expert_blocks(sp, run)
            for q in range(2):
                sp.dma_start(raw[:, q * GW:(q + 1) * GW], d["ple_gate"][q, :, :]).then_inc(s_gw[q], 16)
            sp.wait_ge(s_landed, 1)
            for t in range(NT):
                sp.dma_start(pair_of(t), pair_dram.rearrange("(k t p) c -> t p k c", k=2, p=P)[t, :, :, :])\
                    .then_inc(s_pair[t], 16)
            for q in range(2, 4):
                sp.dma_start(y_flat[:, (q - 2) * GW:(q - 1) * GW], d["ple_gate"][q, :, :]).then_inc(s_gw[q], 16)
            for u in range(2 * NT):
                half, t = u // NT, u % NT
                sp.wait_ge(s_mix, 2 * u + 2)
                sp.dma_start(out[t * P:(t + 1) * P, half * 512:(half + 1) * 512],
                             raw[:, t * DM + half * 512:t * DM + (half + 1) * 512]).then_inc(s_out, 16)
            sp.wait_ge(s_out, 16 * 2 * NT)

        @block.gpsimd
        def _(pool):
            g = nc.gpsimd
            g.memset(ident[:, :], 0.0).then_inc(s_setup, 1)
            g.memset(sel_head[:, :, :], 0.0).then_inc(s_setup, 1)
            g.memset(minus_half, -0.5).then_inc(s_setup, 1)
            for grp in range(NG):
                pool.wait_ge(s_setup, 3 + 2 * grp)
                g.memset(q_scale[0:DA, grp:grp + 1], 2.0 ** (2 * grp - 2)).then_inc(s_setup, 1)
                pool.wait_ge(s_setup, 4 + 2 * grp)
                g.memset(q_scale[DA:P, grp:grp + 1], 2.0 ** (2 * grp - 1)).then_inc(s_setup, 1)
            pool.wait_ge(s_setup, 11)
            g.memset(v_m[:, :, :, P:P + 1], 1.0).then_inc(s_setup, 1)
            g.memset(pre[:, :, 0:3], 0.0).then_inc(s_setup, 1)
            g.iota(dist[:, :], pattern=[[-1, SEQ]], base=384, channel_multiplier=1,
                   allow_small_or_imprecise_dtypes=True).then_inc(s_setup, 1)
            pool.wait_ge(s_setup, 14)
            g.affine_select(out=ident[:, :], in_=ident[:, :], compare_op=ALU.not_equal, fill=1.0, base=0,
                            pattern=[[-1, P]], channel_multiplier=1).then_inc(s_setup, 1)
            g.affine_select(out=sel_head[:, :, :], in_=sel_head[:, :, :], compare_op=ALU.not_equal, fill=1.0,
                            base=0, pattern=[[-1, HM], [0, P]], channel_multiplier=1).then_inc(s_setup, 1)
            g.affine_select(out=mdist[:, 0:P], in_=dist[:, 384:512], compare_op=ALU.is_ge, fill=BIG, base=0,
                            pattern=[[-1, P]], channel_multiplier=1).then_inc(s_md0, 1)

            def split(i):
                pool.wait_ge(s_whi, i + 1)
                r = i % RAWS
                g.tensor_tensor(ring(w_lo, i), raw[:, r * PW:(r + 1) * PW], ring(w_hi, i).bitcast(F32),
                                ALU.subtract).then_inc(s_wlo, 1)

            def split_wide(grp):
                pool.wait_ge(s_widehi, grp + 1)
                g.tensor_tensor(wide(w_lo), wide_raw, wide(w_hi).bitcast(F32), ALU.subtract).then_inc(s_widelo, 1)

            def strike_future():
                for b in range(1, NT):
                    pool.wait_ge(s_acc, HI_ * b)
                    last = score[:, SO[b] + b * P:SO[b] + (b + 1) * P]
                    g.affine_select(out=last, in_=last, compare_op=ALU.is_ge, fill=-BIG, base=0,
                                    pattern=[[-1, P]], channel_multiplier=1).then_inc(s_fut, 1)

            def mask_decay(h):
                pool.wait_ge(s_dexp, h + 1)
                for b in range(NT):
                    own = decay[:, LO_[b]:LO_[b] + P]
                    g.affine_select(out=own, in_=own, compare_op=ALU.is_ge, fill=0.0, base=0,
                                    pattern=[[1, P]], channel_multiplier=-1).then_inc(s_dmask, 1)

            def power(h):
                pool.wait_ge(s_var, h + 1)
                g.tensor_tensor(rstd, den, minus_half, ALU.pow).then_inc(s_pow, 1)

            for i in range(RING):
                split(i)
            for n in range(NSTEP):
                grp, j = kind(n)
                i = piece_at(n)
                if n == SMALL - 1:
                    strike_future()
                if i is not None and i + RING < NPIECE:
                    split(i + RING)
                if grp is not None and j == 1:
                    split_wide(grp)
                if grp and j == 2:
                    power(grp - 1)
                if j == 4 and grp is not None:
                    mask_decay(grp)

            def split_out(q):
                pool.wait_ge(s_ohi, q + 1)
                g.tensor_tensor(group(w_lo, OSLOT[q]), raw[:, ORAW[q]:ORAW[q] + GW].rearrange("p (u c) -> p u c", u=4),
                                group(w_hi, OSLOT[q]).bitcast(F32), ALU.subtract).then_inc(s_olo, 1)

            split_out(0)
            power(NG - 1)
            split_out(1)
            split_out(2)
            pool.wait_ge(s_ym, NG)
            g.memset(tri[:, :], 1.0).then_inc(s_rc, 1)
            g.memset(ones[:, :], 1.0).then_inc(s_rc, 1)
            flags = dict(allow_small_or_imprecise_dtypes=True)
            g.iota(count_c, pattern=[[1, P]], base=0, channel_multiplier=0, **flags).then_inc(s_rc, 1)
            g.iota(rank, pattern=[[-1, EG]], base=EG, channel_multiplier=0, **flags).then_inc(s_rc, 1)
            g.iota(token, pattern=[[P, NT]], base=0, channel_multiplier=1, **flags).then_inc(s_rc, 1)
            g.iota(skip_row, pattern=[[1, 1]], base=SKIP, channel_multiplier=1, **flags).then_inc(s_rc, 1)
            pool.wait_ge(s_rc, 6)
            g.affine_select(out=tri[:, :], in_=tri[:, :], compare_op=ALU.is_gt, fill=0.0, base=0,
                            pattern=[[1, P]], channel_multiplier=-1).then_inc(s_rc, 1)
            split_out(3)

            def inverse(t, ready, done):
                pool.wait_ge(ready, t + 1)
                g.tensor_tensor(rs8[:, t:t + 1], ve8[:, t:t + 1], minus_half[:, 0:1], ALU.pow).then_inc(done, 1)

            for t in range(NT):
                inverse(t, s_ve, s_rs)

            def gather(T, e, par):
                g.tensor_copy(at_got[:, par:par + 1], row_got[:, bass.ds(e, 1)]).then_inc(s_cg, 1)
                wait_count(pool, s_cg, T + 1)
                g.indirect_dma_start(out=x_got[par], out_offset=None, in_=x1_dram[:, :],
                                     in_offset=bass.IndirectOffsetOnAxis(ap=at_got[:, par:par + 1], axis=0),
                                     bounds_check=SEQ - 1, oob_is_err=False).then_inc(s_got[par], 16)

            def scatter(T, e, par):
                wait_count(pool, s_put[par], arrived(T - 2, par))
                g.tensor_copy(at_put[:, par:par + 1], row_put[:, bass.ds(e, 1)]).then_inc(s_cp, 1)
                wait_count(pool, s_cp, T + 1)
                wait_count(pool, s_outa, T + 1)
                wait_count(pool, s_outv, T + 1)
                g.indirect_dma_start(out=pair_dram[:, :],
                                     out_offset=bass.IndirectOffsetOnAxis(ap=at_put[:, par:par + 1], axis=0),
                                     in_=y_out[par], in_offset=None,
                                     bounds_check=2 * SEQ - 1, oob_is_err=False).then_inc(s_put[par], 16)

            def split_down(T, par):
                wait_count(pool, s_ehi2, T + 1)
                at_ = par * EW + 2 * GW
                g.tensor_tensor(w_lo[:, ESLOT[2] * GW:(ESLOT[2] + 1) * GW], raw[:, at_:at_ + GW],
                                w_hi[:, ESLOT[2] * GW:(ESLOT[2] + 1) * GW].bitcast(F32), ALU.subtract)\
                    .then_inc(s_elo2, 1)

            split_down(0, 0)

            def run(b, base):
                wait_count(pool, s_rows, 2 * b + 2)
                if isinstance(b, int):
                    pool.wait_ge(s_x1d, 16 * NT)
                for par in range(2):
                    gather(base + par, par, par)

                def step(e, par, first=False, last=False):
                    T = base + e
                    if not last:
                        wait_count(pool, s_xt, 2 * T + 2)
                        gather(T + 2, e + 2, par)
                    if not (first and isinstance(b, int)):
                        split_down(T, par)
                    if not first:
                        scatter(T - 1, e - 1, 1 - par)

                step(0, 0, first=True)
                step(1, 1)
                with pool.Fori(1, NE // 2 - 1) as i:
                    for par in range(2):
                        step(2 * i + par, par)
                step(NE - 2, 0, last=True)
                step(NE - 1, 1, last=True)
                scatter(base + NE - 1, NE - 1, 1)
                for par in range(2):
                    wait_count(pool, s_put[par], 8 * (base + NE))

            expert_blocks(pool, run)
            g.sem_inc(s_landed, 1)

            def split_gate(q):
                pool.wait_ge(s_ghi, q + 1)
                src = raw[:, q * GW:(q + 1) * GW] if q < 2 else y_flat[:, (q - 2) * GW:(q - 1) * GW]
                g.tensor_tensor(group(w_lo, OSLOT[q]), src.rearrange("p (u c) -> p u c", u=4),
                                group(w_hi, OSLOT[q]).bitcast(F32), ALU.subtract).then_inc(s_glo, 1)

            split_gate(0)
            split_gate(1)
            for t in range(NT):
                inverse(t, s_ve2, s_rs2)
            split_gate(2)

        @block.scalar
        def _(act):
            a = nc.scalar

            def round_piece(i):
                if i >= RING:
                    act.wait_ge(s_proj, step_of(i - RING) + 1)
                r = i % RAWS
                act.wait_ge(s_raw[r], 16 * (i // RAWS + 1))
                a.activation(ring(w_hi, i), raw[:, r * PW:(r + 1) * PW], ACT.Copy).then_inc(s_whi, 1)

            def round_wide(grp):
                if grp:
                    act.wait_ge(s_proj, step_no(grp, 0))
                act.wait_ge(s_wide, 16 * (grp + 1))
                a.activation(wide(w_hi), wide_raw, ACT.Copy).then_inc(s_widehi, 1)

            def evacuate(n):
                act.wait_ge(s_proj, n + 1)
                grp, j = kind(n)
                src = proj_bank[n % 2]
                if grp is None:
                    a.activation(index_hi[:, j, :], src[:, :], ACT.Copy).then_inc(s_evac, 1)
                    return
                par = grp % 2
                if j == 0:
                    if grp >= 2:
                        act.wait_ge(s_qk, 8 * (grp - 1))
                    if grp == 0:
                        act.wait_ge(s_setup, 14)
                    a.activation(q_t[:, par, :], src[:, :], ACT.Identity, scale=q_scale[:, grp:grp + 1])\
                        .then_inc(s_evac, 1)
                elif j == 1:
                    a.activation(k_t[:, par, :], src[:, :], ACT.Copy).then_inc(s_evac, 1)
                elif j < TALL:
                    if grp >= 1:
                        act.wait_ge(s_cacc, 8 * grp)
                    a.activation(pre[:, j - 2, 3:515], src[:, :], ACT.Copy).then_inc(s_evac, 1)
                else:
                    t = j - TALL
                    if grp >= 2:
                        act.wait_ge(s_pv, 8 * (grp - 1))
                        act.wait_ge(s_mnum, grp - 1)
                        act.wait_ge(s_ym, grp - 1)
                    a.activation(v_a[:, par, t, :], src[:, 0:P], ACT.Copy)
                    a.activation(v_m[:, par, t, 0:P], src[:, P:2 * P], ACT.Copy)
                    a.activation(o_m[:, par, t, :], src[:, 2 * P:WIDE], ACT.Tanh, scale=0.5).then_inc(s_evac, 1)

            def gates():
                act.wait_ge(s_row_v, 3)
                a.activation(c_row, c_row, ACT.Exp, scale=-1.0).then_inc(s_row_a, 1)
                act.wait_ge(s_row_a, 1)
                a.activation(c_row, c_row, ACT.Ln, bias=1.0).then_inc(s_row_a, 1)
                act.wait_ge(s_row_v, 10)
                a.activation(g_row, c_row, ACT.Exp, scale=-1.0).then_inc(s_row_a, 1)

            def index_relu():
                for n in range(3 * HI_):
                    b, h = n // HI_ + 1, n % HI_
                    act.wait_ge(s_idx, n + 1)
                    if n >= 2:
                        act.wait_ge(s_acc, n - 1)
                    a.activation(relu[:, n % 2, 0:(b + 1) * P], index_bank[n % 4][:, 0:(b + 1) * P], ACT.Relu,
                                 scale=DI ** -0.5).then_inc(s_relu, 1)

            def softmax(g, u):
                U, h, b = 8 * g + u, 2 * g + u // NT, u % NT
                act.wait_ge(s_negmax, U + 1)
                if U >= 2:
                    act.wait_ge(s_turn, U - 1)
                if u == 0 and g >= 1:
                    act.wait_ge(s_yinv, g)
                a.activation(prob[:, U % 2, 0:(b + 1) * P], masked[:, U % 2, 0:(b + 1) * P], ACT.Exp,
                             scale=2.0 ** -(h + 1), bias=neg_max[:, U % 2:U % 2 + 1],
                             accum_out=row_sum[:, b, u // NT:u // NT + 1]).then_inc(s_exp, 1)

            def lstm_exp(h):
                act.wait_ge(s_gadd, 4 * (h + 1))
                a.activation(decay[:, :], decay[:, :], ACT.Exp).then_inc(s_dexp, 1)

            def lstm_hidden(h):
                act.wait_ge(s_mnum, h + 1)
                if h >= 1:
                    act.wait_ge(s_ym, h)
                for half in range(2):
                    a.activation(hidden[:, 2 * half:2 * half + 2, :],
                                 lstm_bank[half][:, 0:258].rearrange("p (s c) -> p s c", s=2), ACT.Copy)\
                        .then_inc(s_hid, 1)

            def conv_tanh(h, c):
                act.wait_ge(s_cacc, 8 * h + 4 * c + 4)
                if 2 * h + c >= 1:
                    act.wait_ge(s_conv, 2 * h + c)
                a.activation(tanh_c, conv[:, c, :], ACT.Tanh, scale=0.5).then_inc(s_ctanh, 1)

            def attention(g, j):
                if j < 4:
                    softmax(g, 2 * j)
                    softmax(g, 2 * j + 1)

            def work(g, j):
                if g < NG:
                    if j == 4:
                        lstm_exp(g)
                    if j in (4, 5):
                        conv_tanh(g, j - 4)
                if g and j == 1:
                    lstm_hidden(g - 1)
                if g and j < 4:
                    attention(g - 1, j + 2)
                if g < NG and j >= 6:
                    attention(g, j - 6)

            def round_x(c):
                act.wait_ge(s_x[c], 16)
                a.activation(a_hi[:, 2 * c:2 * c + 2, :], x_raw[:, 2 * c:2 * c + 2, :], ACT.Copy).then_inc(s_xhi, 1)

            round_x(0)
            round_piece(0)
            round_x(1)
            round_x(2)
            round_x(3)
            act.wait_ge(s_w16, 16)
            a.activation(w16_hi[:, :, :], w16[:, :, :], ACT.Copy).then_inc(s_w16s, 1)
            for i in range(1, RING):
                round_piece(i)
            for n in range(NSTEP):
                grp, j = kind(n)
                evacuate(n)
                if n == SMALL - 1:
                    gates()
                    index_relu()
                i = piece_at(n)
                if i is not None and i + RING < NPIECE:
                    round_piece(i + RING)
                if grp is not None and j == 1:
                    round_wide(grp)
                if grp is not None:
                    work(grp, j)

            def round_out(q):
                act.wait_ge(s_or[q], 16)
                if q < 3:
                    act.wait_ge(s_proj, NSTEP)
                else:
                    act.wait_ge(s_wo, 1)
                a.activation(group(w_hi, OSLOT[q]), raw[:, ORAW[q]:ORAW[q] + GW].rearrange("p (u c) -> p u c", u=4),
                             ACT.Copy).then_inc(s_ohi, 1)

            for j in range(NG):
                work(NG, j)
                for half in range(2):
                    act.wait_ge(s_yt, 2 * j + half + 1)
                    a.activation(a_hi[:, 4 * half + j, :], proj_bank[half][:, :], ACT.Copy).then_inc(s_yhi, 1)
                if j < 3:
                    round_out(j)
            round_out(3)
            act.wait_ge(s_wr, 16)
            act.wait_ge(s_wo, 2)
            a.activation(w_hi[:, WR_AT:3 * GW], wr_raw.rearrange("p k c -> p (k c)"), ACT.Copy).then_inc(s_wrs, 1)

            def round_expert(T, par, q, free=None):
                act.wait_ge(s_ew[par][q], arrived(T, par))
                if free is not None:
                    act.wait_ge(*free)
                else:
                    act.wait_ge(*((s_gu, 2 * T - 1 + q) if q < 2 else (s_dn, T)))
                a.activation(group(w_hi, ESLOT[q]),
                             raw[:, par * EW + q * GW:par * EW + (q + 1) * GW].rearrange("p (u c) -> p u c", u=4),
                             ACT.Copy).then_inc(s_ehi if q < 2 else s_ehi2, 1)

            round_expert(0, 0, 0, (s_wot, NT))
            for u in range(2 * NT):
                t, half = u // 2, u % 2
                act.wait_ge(s_x1t, u + 1)
                a.activation(a_hi[:, 4 * half:4 * half + 4, t * P:(t + 1) * P],
                             turned_1[u % 4][:, :].rearrange("p (k c) -> p k c", k=4), ACT.Copy).then_inc(s_x1hi, 1)
            round_expert(0, 0, 1, (s_wo, 3))
            round_expert(0, 0, 2, (s_rp, 1))
            act.wait_ge(s_rt, RT_GROUP)
            a.activation(dif_g, dif_g, ACT.Exp).then_inc(s_ra, 1)
            act.wait_ge(s_rt, RT_SECOND)
            a.activation(col[5], col[5], ACT.Exp).then_inc(s_ra, 1)

            def ple_out(u):
                act.wait_ge(s_pp, u + 1)
                a.activation(ple[:, u // 2, (u % 2) * 512:(u % 2 + 1) * 512], bank[u % 4][:, :], ACT.Copy)\
                    .then_inc(s_pev, 1)

            def tokens_hi(T, par, half):
                act.wait_ge(s_xt, 2 * T + half + 1)
                a.activation(xg(hi_flat, par)[:, 4 * half:4 * half + 4, :],
                             bank[2 + half][:, :].rearrange("p (k c) -> p k c", k=4), ACT.Copy).then_inc(s_xh, 1)

            def run(b, base):
                if not isinstance(b, int):
                    for q in range(2):
                        round_expert(base, 0, q)
                for half in range(2):
                    tokens_hi(base, 0, half)

                def hidden_hi(T):
                    act.wait_ge(s_th, T + 1)
                    a.activation(ht(hi_flat), bank[1][:, 0:DE].rearrange("p (k c) -> p k c", k=2), ACT.Copy)\
                        .then_inc(s_hh, 1)

                def put_out(T, par):
                    act.wait_ge(s_dn, T + 1)
                    wait_count(act, s_put[par], arrived(T - 2, par))
                    a.activation(y_out[par][:, 0:512], bank[4][:, :], ACT.Copy).then_inc(s_outa, 1)

                def step(T, par, first=False, last=False):
                    if not first:
                        hidden_hi(T - 1)
                    if not last:
                        round_expert(T + 1, 1 - par, 0)
                    act.wait_ge(s_gu, 2 * T + 2)
                    wait_count(act, s_h, T)
                    a.activation(silu_g, gu_bank[par][:, 0:DE], ACT.Silu).then_inc(s_silu, 1)
                    if not last:
                        tokens_hi(T + 1, 1 - par, 0)
                        tokens_hi(T + 1, 1 - par, 1)
                        round_expert(T + 1, 1 - par, 1)
                    if not first:
                        put_out(T - 1, 1 - par)
                    if not (first and isinstance(b, int)):
                        round_expert(T, par, 2)

                step(base, 0, first=True)
                step(base + 1, 1)
                with act.Fori(1, NE // 2 - 1) as i:
                    for par in range(2):
                        step(base + 2 * i + par, par)
                step(base + NE - 2, 0)
                step(base + NE - 1, 1, last=True)
                hidden_hi(base + NE - 1)
                put_out(base + NE - 1, 1)

            expert_blocks(act, run)

            def round_gate(q):
                act.wait_ge(s_gw[q], 16)
                if q == 3:
                    act.wait_ge(s_gt, NT)
                src = raw[:, q * GW:(q + 1) * GW] if q < 2 else y_flat[:, (q - 2) * GW:(q - 1) * GW]
                a.activation(group(w_hi, OSLOT[q]), src.rearrange("p (u c) -> p u c", u=4), ACT.Copy)\
                    .then_inc(s_ghi, 1)

            act.wait_ge(s_pr, 16)
            a.activation(a_hi[:, 0:2, :], p_raw, ACT.Copy).then_inc(s_phi, 1)
            act.wait_ge(s_pw, 16)
            a.activation(w_hi[:, 0:GW], proj_raw, ACT.Copy).then_inc(s_phi, 1)
            round_gate(0)
            act.wait_ge(s_plo, 2)
            for u in range(2 * NT):
                if u == 4:
                    round_gate(1)
                ple_out(u)
            for u in range(2 * NT):
                t, half = u // 2, u % 2
                if u == 4:
                    round_gate(2)
                act.wait_ge(s_x2t, u + 1)
                a.activation(a_hi[:, 4 * half:4 * half + 4, t * P:(t + 1) * P],
                             turned_2[u % 4][:, :].rearrange("p (k c) -> p k c", k=4), ACT.Copy).then_inc(s_x2hi, 1)
            round_gate(3)
            for u in range(2 * NT):
                half, t = u // NT, u % NT
                act.wait_ge(s_gt, u + 1)
                a.activation(raw[:, t * DM + half * 512:t * DM + (half + 1) * 512],
                             bank[4 * (1 - half) + t][:, :], ACT.Sigmoid).then_inc(s_sig, 1)

        @block.vector
        def _(dve):
            v = nc.vector
            for c in range(4):
                dve.wait_ge(s_xhi, c + 1)
                v.tensor_tensor(a_lo[:, 2 * c:2 * c + 2, :], x_raw[:, 2 * c:2 * c + 2, :],
                                a_hi[:, 2 * c:2 * c + 2, :].bitcast(F32), ALU.subtract).then_inc(s_xlo, 1)
            dve.wait_ge(s_w16s, 1)
            v.tensor_tensor(w16_lo[:, :, :], w16[:, :, :], w16_hi[:, :, :].bitcast(F32), ALU.subtract)\
                .then_inc(s_w16s, 1)

            def index_low(n):
                dve.wait_ge(s_evac, n + 1)
                v.tensor_tensor(index_lo[:, n, :], proj_bank[n % 2][:, :], index_hi[:, n, :].bitcast(F32),
                                ALU.subtract).then_inc(s_ilo, 1)

            def gates():
                index_low(0)
                index_low(1)
                dve.wait_ge(s_gate_p, 1)
                pre16 = lstm_bank[0][:, 0:64].rearrange("p (s c) -> p s c", s=NT)
                v.tensor_scalar(w_head[:, :, :], pre16[:, :, 0:8], HI_ ** -0.5, None, ALU.mult).then_inc(s_gate_e, 1)
                dve.wait_ge(s_const, 48)
                v.tensor_tensor(if_pre[:, :, :], pre16[:, :, 8:16],
                                if_bias[:, :].unsqueeze(1).broadcast_to([P, NT, 8]), ALU.add).then_inc(s_gate_e, 1)
                v.tensor_scalar(gn_half[:, :], gn_half[:, :], 0.5, None, ALU.mult).then_inc(s_gate_e, 1)
                dve.wait_ge(s_row_p, 1)
                v.tensor_copy(i_row, lstm_bank[1][0:HM, :]).then_inc(s_row_v, 1)
                v.tensor_copy(f_row, turn_bank[0:HM, :]).then_inc(s_row_v, 1)
                dve.wait_ge(s_row_v, 2)
                v.scalar_tensor_tensor(out=c_row, in0=f_row, scalar=-1.0, in1=f_row, op0=ALU.mult,
                                       op1=ALU.max).then_inc(s_row_v, 1)
                v.memset(g_row, 1.0).then_inc(s_row_v, 1)
                index_low(2)
                dve.wait_ge(s_row_a, 2)
                v.scalar_tensor_tensor(out=f_row, in0=f_row, scalar=0.0, in1=c_row, op0=ALU.min,
                                       op1=ALU.subtract).then_inc(s_row_v, 1)
                dve.wait_ge(s_row_v, 5)
                v.tensor_tensor_scan(c_row, g_row, f_row, 0.0, ALU.mult, ALU.add).then_inc(s_row_v, 1)
                dve.wait_ge(s_row_v, 6)
                v.tensor_tensor(i_row, i_row, c_row, ALU.subtract).then_inc(s_row_v, 1)
                dve.wait_ge(s_row_v, 7)
                v.tensor_tensor_scan(g_row, i_row, i_row, 0.0, ALU.max, ALU.max).then_inc(s_row_v, 1)
                dve.wait_ge(s_row_v, 8)
                v.tensor_tensor(c_row, c_row, g_row, ALU.add).then_inc(s_row_v, 1)
                v.tensor_scalar(nega_row, g_row, -1.0, None, ALU.mult).then_inc(s_row_v, 1)

            def gate_columns():
                dve.wait_ge(s_col_p, 2)
                cols = lstm_bank[0][:, 0:32].rearrange("p (k s h) -> p k s h", k=2, s=NT)
                v.tensor_copy(a_col[:, :, :], cols[:, 0, :, :]).then_inc(s_col_v, 1)
                v.tensor_copy(em_col[:, :, :], cols[:, 1, :, :]).then_inc(s_col_v, 1)

            def index_sum():
                for n in range(3 * HI_):
                    b, h = n // HI_ + 1, n % HI_
                    dve.wait_ge(s_relu, n + 1)
                    acc = score[:, SO[b]:SO[b] + (b + 1) * P]
                    w = w_head[:, b, h:h + 1]
                    r = relu[:, n % 2, 0:(b + 1) * P]
                    if h == 0:
                        v.tensor_scalar(acc, r, w, None, ALU.mult).then_inc(s_acc, 1)
                    else:
                        dve.wait_ge(s_acc, n)
                        v.scalar_tensor_tensor(out=acc, in0=r, scalar=w, in1=acc, op0=ALU.mult, op1=ALU.add)\
                            .then_inc(s_acc, 1)

            def top_keys():
                dve.wait_ge(s_fut, 3)
                n = 0
                for r in range(TOPK // 8):
                    for b in range(1, NT):
                        src = (score if r == 0 else left)[:, SO[b]:SO[b] + (b + 1) * P]
                        if r:
                            dve.wait_ge(s_top, 6 * (r - 1) + 3 + b)
                        v.max(best[:, b - 1, :], src).then_inc(s_top, 1)
                    for b in range(1, NT):
                        src = (score if r == 0 else left)[:, SO[b]:SO[b] + (b + 1) * P]
                        dve.wait_ge(s_top, 6 * r + b)
                        v.match_replace(left[:, SO[b]:SO[b] + (b + 1) * P], best[:, b - 1, :], src, TAKEN)\
                            .then_inc(s_top, 1)
                    if r == 4:
                        gate_columns()
                        dve.wait_ge(s_gate_e, GATE_E)
                    if r == 9:
                        lstm_add(0)
                    if r in (11, 13):
                        convolve(0, (r - 11) // 2)
                dve.wait_ge(s_top, 6 * (TOPK // 8))
                for b in range(1, NT):
                    part = left[:, SO[b]:SO[b] + (b + 1) * P]
                    v.tensor_scalar(part, part, TAKEN / 10, BIG, ALU.is_ge, ALU.mult).then_inc(s_mdist, 1)
                for b in range(1, NT):
                    dve.wait_ge(s_mdist, b)
                    v.tensor_tensor(mdist[:, MO[b]:MO[b] + (b + 1) * P], left[:, SO[b]:SO[b] + (b + 1) * P],
                                    dist[:, (3 - b) * P:SEQ], ALU.add).then_inc(s_mdist, 1)
                dve.wait_ge(s_md0, 1)
                dve.wait_ge(s_mdist, 6)

            def mask_scores(g, u):
                U, h, b = 8 * g + u, 2 * g + u // NT, u % NT
                dve.wait_ge(s_qk, U + 1)
                if U >= 2:
                    dve.wait_ge(s_exp, U - 1)
                n = (b + 1) * P
                v.tensor_tensor_reduce(out=masked[:, U % 2, 0:n], in0=score_bank[U % 2][:, 0:n],
                                       in1=mdist[:, MO[b]:MO[b] + n], scale=1.0, scalar=-3.0e38,
                                       op0=ALU.subtract, op1=ALU.max,
                                       accum_out=row_max[:, U % 2:U % 2 + 1]).then_inc(s_masked, 1)
                dve.wait_ge(s_masked, U + 1)
                v.tensor_scalar(neg_max[:, U % 2:U % 2 + 1], row_max[:, U % 2:U % 2 + 1], -(2.0 ** -(h + 1)), None,
                                ALU.mult).then_inc(s_negmax, 1)

            def copy_turned(g, u):
                U, n = 8 * g + u, (u % NT + 1) * P
                dve.wait_ge(s_turn, U + 1)
                if U >= 2:
                    dve.wait_ge(s_pv, U - 1)
                v.tensor_copy(prob_t[:, U % 2, 0:n], turn_bank[:, 0:n]).then_inc(s_probt, 1)

            def attn_out(g):
                dve.wait_ge(s_pv, 8 * (g + 1))
                dve.wait_ge(s_exp, 8 * (g + 1))
                if g:
                    dve.wait_ge(s_ya, g)
                v.reciprocal(row_inv, row_sum).then_inc(s_yinv, 1)
                dve.wait_ge(s_yinv, g + 1)
                v.tensor_tensor(y[:, :, g * P:(g + 1) * P].rearrange("p t (h c) -> p t h c", h=2),
                                attn_bank[:, :].rearrange("p (t h c) -> p t h c", t=NT, h=2),
                                row_inv.unsqueeze(3).broadcast_to([P, NT, 2, DA]), ALU.mult).then_inc(s_ya, 1)

            def lstm_add(h):
                dve.wait_ge(s_gbc, h + 1)
                if h:
                    dve.wait_ge(s_mw, 4 * h)
                else:
                    dve.wait_ge(s_xlo, 4)
                for b in range(NT):
                    v.tensor_scalar(decay[:, LO_[b]:LO_[b + 1]], lstm_bank[1][:, b * P:SEQ],
                                    a_col[:, b, h:h + 1], 0.0, ALU.add, ALU.min).then_inc(s_gadd, 1)

            def lstm_weight(h, b):
                dve.wait_ge(s_mqk, 4 * h + b + 1)
                dve.wait_ge(s_dmask, 4 * (h + 1))
                if h:
                    dve.wait_ge(s_mnum, h)
                v.scalar_tensor_tensor(out=weight[:, LO_[b]:LO_[b + 1]],
                                       in0=lstm_bank[b % 2][:, 0:SEQ - b * P], scalar=0.25 * P ** -0.5,
                                       in1=decay[:, LO_[b]:LO_[b + 1]], op0=ALU.mult, op1=ALU.mult)\
                    .then_inc(s_mw, 1)

            def convolve(h, c):
                w = conv_wb[:, 4 * c + h, :]
                dve.wait_ge(s_evac, step_no(h, 2 + c) + 1)
                n = 8 * h + 4 * c
                if 2 * h + c >= 2:
                    dve.wait_ge(s_conv, 2 * h + c - 1)
                v.tensor_scalar(conv[:, c, :], pre[:, c, 0:SEQ], w[:, 0:1], w[:, 4:5], ALU.mult, ALU.add)\
                    .then_inc(s_cacc, 1)
                for tap in range(1, 4):
                    dve.wait_ge(s_cacc, n + tap)
                    v.scalar_tensor_tensor(out=conv[:, c, :], in0=pre[:, c, tap:tap + SEQ], scalar=w[:, tap:tap + 1],
                                           in1=conv[:, c, :], op0=ALU.mult, op1=ALU.add).then_inc(s_cacc, 1)
                dve.wait_ge(s_ctanh, 2 * h + c + 1)
                if h:
                    dve.wait_ge(s_mqk, 4 * h)
                v.scalar_tensor_tensor(out=qk_m[:, c, :], in0=tanh_c, scalar=1.0, in1=conv[:, c, :], op0=ALU.add,
                                       op1=ALU.mult).then_inc(s_conv, 1)

            POST = 17

            def lstm_out(h):
                n = [POST * h]

                def step(ins):
                    n[0] += 1
                    ins.then_inc(s_post, 1)

                def settle():
                    dve.wait_ge(s_post, n[0])

                dve.wait_ge(s_hid, 2 * (h + 1))
                if h:
                    dve.wait_ge(s_pow, h)
                raw_den = hidden[:, :, P:P + 1].squeeze(2)
                step(v.scalar_tensor_tensor(out=den, in0=raw_den, scalar=-1.0, in1=raw_den, op0=ALU.mult,
                                            op1=ALU.max))
                settle()
                step(v.tensor_tensor(den, den, em_col[:, :, h], ALU.max))
                settle()
                step(v.reciprocal(den_inv, den))
                settle()
                hid = hidden[:, :, 0:P]
                step(v.tensor_tensor(hid, hid, den_inv.unsqueeze(2).broadcast_to([P, NT, P]), ALU.mult))
                settle()
                for t in range(NT):
                    step(v.bn_stats(stats[:, t, :], hid[:, t, :]))
                settle()
                for t in range(NT):
                    step(v.bn_aggr(mean_var[:, t, :], stats[:, t, :]))
                settle()
                v.tensor_scalar(den, mean_var[:, :, 1:2].squeeze(2), EPS, None, ALU.add).then_inc(s_var, 1)
                dve.wait_ge(s_pow, h + 1)
                for t in range(NT):
                    step(v.tensor_scalar(hid[:, t, :], hid[:, t, :], mean_var[:, t, 0:1], rstd[:, t:t + 1],
                                         ALU.subtract, ALU.mult))
                settle()
                step(v.tensor_tensor(hid, hid, gn_half[:, h * P:(h + 1) * P].unsqueeze(1).broadcast_to([P, NT, P]),
                                     ALU.mult))
                settle()
                assert n[0] == POST * (h + 1), n
                v.scalar_tensor_tensor(out=y[:, :, (4 + h) * P:(5 + h) * P], in0=o_m[:, h % 2, :, :], scalar=1.0,
                                       in1=hid, op0=ALU.add, op1=ALU.mult).then_inc(s_ym, 1)

            def attention(g, j):
                for e in range(2):
                    if j < 4:
                        mask_scores(g, 2 * j + e)
                    if 1 <= j <= 4:
                        copy_turned(g, 2 * j - 2 + e)
                if j == 5:
                    attn_out(g)

            def work(g, j):
                if g and j < 4:
                    attention(g - 1, j + 2)
                if g < NG:
                    if j == 3 and g:
                        lstm_add(g)
                        convolve(g, 0)
                    if j == 4 and g:
                        convolve(g, 1)
                    if j >= 6:
                        lstm_weight(g, 2 * j - 12)
                        lstm_weight(g, 2 * j - 11)
                    if j >= 6:
                        attention(g, j - 6)
                if g and j == 2:
                    lstm_out(g - 1)

            gates()
            index_sum()
            top_keys()
            for g in range(NG):
                for j in range(STEPS):
                    work(g, j)
            for j in range(NG):
                work(NG, j)
                for half in range(2):
                    dve.wait_ge(s_yhi, 2 * j + half + 1)
                    k = 4 * half + j
                    v.tensor_tensor(a_lo[:, k, :], proj_bank[half][:, :], a_hi[:, k, :].bitcast(F32),
                                    ALU.subtract).then_inc(s_ylo, 1)
            def residual(t, half):
                r = mine[:, t, half * 512:(half + 1) * 512]
                v.scalar_tensor_tensor(out=r, in0=r, scalar=ALPHA, in1=bank[4 * (1 - half) + t][:, :],
                                       op0=ALU.mult, op1=ALU.add).then_inc(s_r, 1)

            def norm_stats(t, half, count):
                v.bn_stats(stat8[:, t, 6 * half:6 * half + 6], mine[:, t, half * 512:(half + 1) * 512])\
                    .then_inc(count, 1)

            def norm_variance(t, count, base, done):
                dve.wait_ge(count, base)
                v.bn_aggr(mv8[:, t, :], stat8[:, t, :]).then_inc(count, 1)
                dve.wait_ge(count, base + 1)
                v.tensor_scalar(ve8[:, t:t + 1], mv8[:, t, 1:2], EPS, None, ALU.add).then_inc(done, 1)

            def norm_apply(t, done):
                m = mine[:, t, :]
                v.scalar_tensor_tensor(out=m, in0=m, scalar=mv8[:, t, 0:1], in1=ln_g, op0=ALU.subtract,
                                       op1=ALU.mult).then_inc(done, 1)
                dve.wait_ge(done, 2 * t + 1)
                v.scalar_tensor_tensor(out=m, in0=m, scalar=rs8[:, t:t + 1], in1=ln_b, op0=ALU.mult,
                                       op1=ALU.add).then_inc(done, 1)

            def turned_low(u, banks, hi, lo):
                t, half = u // 2, u % 2
                dve.wait_ge(hi, u + 1)
                v.tensor_tensor(a_lo[:, 4 * half:4 * half + 4, t * P:(t + 1) * P],
                                banks[u % 4][:, :].rearrange("p (k c) -> p k c", k=4),
                                a_hi[:, 4 * half:4 * half + 4, t * P:(t + 1) * P].bitcast(F32), ALU.subtract)\
                    .then_inc(lo, 1)

            def norm_tiles(prepare, ready, done, weights, banks, hi, lo):
                for t in range(NT + 1):
                    if t < NT:
                        prepare(t)
                    if t:
                        if t == 1:
                            dve.wait_ge(weights, 32)
                        dve.wait_ge(ready, t)
                        norm_apply(t - 1, done)
                    if t >= 2:
                        turned_low(2 * t - 4, banks, hi, lo)
                        turned_low(2 * t - 3, banks, hi, lo)
                turned_low(2 * NT - 2, banks, hi, lo)
                turned_low(2 * NT - 1, banks, hi, lo)

            dve.wait_ge(s_wo, 2)
            for t in range(NT):
                dve.wait_ge(s_xn[t], 16)
                residual(t, 0)
            for t in range(NT):
                dve.wait_ge(s_r, t + 1)
                norm_stats(t, 0, s_bn)
            dve.wait_ge(s_wrs, 1)
            v.tensor_tensor(w_lo[:, WR_AT:3 * GW], wr_raw.rearrange("p k c -> p (k c)"),
                            w_hi[:, WR_AT:3 * GW].bitcast(F32), ALU.subtract).then_inc(s_wrs, 1)

            def mixed(t):
                dve.wait_ge(s_wot, t + 1)
                residual(t, 1)
                dve.wait_ge(s_r, NT + t + 1)
                norm_stats(t, 1, s_bn)
                norm_variance(t, s_bn, NT + 2 * t + 1, s_ve)

            norm_tiles(mixed, s_rs, s_ln, s_lnw, turned_1, s_x1hi, s_x1lo)

            def split_expert(T, par, q):
                dve.wait_ge(s_ehi, 2 * T + q + 1)
                v.tensor_tensor(group(w_lo, ESLOT[q]),
                                raw[:, par * EW + q * GW:par * EW + (q + 1) * GW].rearrange("p (u c) -> p u c", u=4),
                                group(w_hi, ESLOT[q]).bitcast(F32), ALU.subtract).then_inc(s_elo, 1)

            split_expert(0, 0, 0)
            split_expert(0, 0, 1)

            n = [0]

            def step(ins):
                n[0] += 1
                ins.then_inc(s_rt, 1)

            def settle():
                dve.wait_ge(s_rt, n[0])

            def spread(x, k):
                return x.unsqueeze(2).broadcast_to([P, NT, k])

            def top(out, o, k):
                eq = eq_g if k == GROUPS else eq_e
                step(v.tensor_reduce(col[0], o, AXX, ALU.max))
                settle()
                step(v.tensor_tensor(eq, o, spread(col[0], k), ALU.is_equal))
                settle()
                step(v.tensor_tensor(eq, eq, rank[:, 0:k].unsqueeze(1).broadcast_to([P, NT, k]), ALU.mult))
                settle()
                step(v.tensor_reduce(col[1], eq, AXX, ALU.max))
                settle()
                step(v.tensor_tensor(out, eq, spread(col[1], k), ALU.is_equal))
                settle()

            dve.wait_ge(s_rp, 1)
            dve.wait_ge(s_rb, 16)
            dve.wait_ge(s_rc, 7)
            step(v.tensor_tensor(logit, bank[4][:, 0:NT * 36].rearrange("p (t c) -> p t c", t=NT),
                                 r_bias.unsqueeze(1).broadcast_to([P, NT, 36]), ALU.add))
            settle()
            g_logit = logit[:, :, 0:GROUPS]
            top(one_g, g_logit, GROUPS)
            step(v.tensor_tensor(dif_g, g_logit, spread(col[0], GROUPS), ALU.subtract))
            assert n[0] == RT_GROUP, n
            step(v.tensor_tensor(picked, logit[:, :, GROUPS:36].rearrange("p t (g e) -> p t e g", g=GROUPS),
                                 one_g.unsqueeze(2).broadcast_to([P, NT, EG, GROUPS]), ALU.mult))
            settle()
            step(v.tensor_reduce(e_log, picked, AXX, ALU.add))
            settle()
            top(one_e[0], e_log, EG)
            step(v.tensor_copy(col[2], col[0]))
            step(v.scalar_tensor_tensor(out=e_log, in0=one_e[0], scalar=TAKEN, in1=e_log, op0=ALU.mult, op1=ALU.add))
            settle()
            top(one_e[1], e_log, EG)
            step(v.tensor_tensor(col[5], col[0], col[2], ALU.subtract))
            assert n[0] == RT_SECOND, n
            for k in range(2):
                step(v.tensor_tensor(one[k].rearrange("p t (g e) -> p t g e", g=GROUPS),
                                     one_g.unsqueeze(3).broadcast_to([P, NT, GROUPS, EG]),
                                     one_e[k].unsqueeze(2).broadcast_to([P, NT, GROUPS, EG]), ALU.mult))
            settle()
            v.tensor_tensor(chosen[:, :, :], one[0], one[1], ALU.add).then_inc(s_cho, 1)
            for k in range(2):
                step(v.tensor_tensor(tok[k], one[k], spread(token, NE), ALU.mult))
            step(v.tensor_scalar(twice, one[1], 2.0, None, ALU.mult))
            dve.wait_ge(s_ra, 2)
            step(v.tensor_reduce(col[6], dif_g, AXX, ALU.add))
            step(v.tensor_scalar(col[7], col[5], 1.0, None, ALU.add))
            settle()
            step(v.tensor_tensor(col[6], col[6], col[7], ALU.mult))
            settle()
            step(v.reciprocal(gate_w[0], col[6]))
            settle()
            step(v.tensor_tensor(gate_w[1], gate_w[0], col[5], ALU.mult))
            dve.wait_ge(s_pos, 1)
            v.tensor_reduce(most[:, :], bank[6][:, NT * NE:(NT + 1) * NE], AXX, ALU.max).then_inc(s_most, 1)
            for k in range(2):
                settle()
                step(v.tensor_tensor(place, one[k], bank[6][:, 0:NT * NE].rearrange("p (t e) -> p t e", t=NT),
                                     ALU.mult))
                settle()
                step(v.tensor_reduce(col[8 + k], place, AXX, ALU.add))
            settle()

            def tables(b):
                m = [TB * b]

                def tb(ins):
                    m[0] = m[0] + 1
                    ins.then_inc(s_tb, 1)

                def tb_settle():
                    dve.wait_ge(s_tb, m[0])

                for k in range(2):
                    tb(v.tensor_scalar(col[8 + k], col[8 + k], 0.0 if isinstance(b, int) else -float(P), None,
                                       ALU.add))
                tb_settle()
                for k in range(2):
                    tb(v.tensor_tensor(seat[k], count_c.unsqueeze(1).broadcast_to([P, NT, P]), spread(col[8 + k], P),
                                       ALU.is_equal))
                dve.wait_ge(s_tabp, b + 1)
                got, nth = bank[7][:, 0:NE], bank[7][:, NE:2 * NE]
                skip = place.rearrange("p t e -> p (t e)")[:, 0:NE]
                both = place.rearrange("p t e -> p (t e)")[:, NE:2 * NE]
                pick = place.rearrange("p t e -> p (t e)")[:, 2 * NE:3 * NE]
                tb(v.tensor_scalar(skip, nth, 0.0, skip_row, ALU.is_equal, ALU.mult))
                tb(v.tensor_scalar(both, nth, float(SEQ), -float(SEQ), ALU.mult, ALU.add))
                tb(v.tensor_copy(pick, got))
                tb_settle()
                tb(v.tensor_tensor(both, both, pick, ALU.add))
                tb(v.tensor_tensor(pick, pick, skip, ALU.add))
                tb_settle()
                v.tensor_copy(row_got[:, :], pick).then_inc(s_rows, 1)
                v.tensor_tensor(row_put[:, :], both, skip, ALU.add).then_inc(s_rows, 1)

            def tokens_low(T, par, half):
                dve.wait_ge(s_xh, 2 * T + half + 1)
                v.tensor_tensor(xg(lo_flat, par)[:, 4 * half:4 * half + 4, :],
                                bank[2 + half][:, :].rearrange("p (k c) -> p k c", k=4),
                                xg(hi_flat, par)[:, 4 * half:4 * half + 4, :].bitcast(F32), ALU.subtract)\
                    .then_inc(s_xl, 1)


            def run(b, base):
                if not isinstance(b, int):
                    dve.wait_ge(s_cg, base)
                    dve.wait_ge(s_cp, base)
                tables(b)
                if not isinstance(b, int):
                    for q in range(2):
                        split_expert(base, 0, q)
                for half in range(2):
                    tokens_low(base, 0, half)

                def hidden_low(T):
                    dve.wait_ge(s_hh, T + 1)
                    v.tensor_tensor(ht(lo_flat), bank[1][:, 0:DE].rearrange("p (k c) -> p k c", k=2),
                                    ht(hi_flat).bitcast(F32), ALU.subtract).then_inc(s_hl, 1)

                def put_out(T, par):
                    dve.wait_ge(s_dn, T + 1)
                    wait_count(dve, s_put[par], arrived(T - 2, par))
                    v.tensor_copy(y_out[par][:, 512:1024], bank[5][:, :]).then_inc(s_outv, 1)

                def step(T, par, first=False, last=False):
                    if not first:
                        hidden_low(T - 1)
                    if not last:
                        split_expert(T + 1, 1 - par, 0)
                    dve.wait_ge(s_silu, T + 1)
                    wait_count(dve, s_th, T)
                    v.tensor_tensor(h_buf, silu_g, gu_bank[par][:, DE:2 * DE], ALU.mult).then_inc(s_h, 1)
                    if not last:
                        tokens_low(T + 1, 1 - par, 0)
                        tokens_low(T + 1, 1 - par, 1)
                    if not first:
                        put_out(T - 1, 1 - par)
                    if not last:
                        split_expert(T + 1, 1 - par, 1)

                step(base, 0, first=True)
                step(base + 1, 1)
                with dve.Fori(1, NE // 2 - 1) as i:
                    for par in range(2):
                        step(base + 2 * i + par, par)
                step(base + NE - 2, 0)
                step(base + NE - 1, 1, last=True)
                hidden_low(base + NE - 1)
                put_out(base + NE - 1, 1)

            expert_blocks(dve, run)

            dve.wait_ge(s_phi, 1)
            v.tensor_tensor(a_lo[:, 0:2, :], p_raw, a_hi[:, 0:2, :].bitcast(F32), ALU.subtract).then_inc(s_plo, 1)
            dve.wait_ge(s_phi, 2)
            v.tensor_tensor(w_lo[:, 0:GW], proj_raw, w_hi[:, 0:GW].bitcast(F32), ALU.subtract).then_inc(s_plo, 1)
            for t in range(NT):
                v.tensor_scalar(mine[:, t, :], mine[:, t, :], ALPHA, None, ALU.mult).then_inc(s_r2, 1)

            def expert_sum(t):
                dve.wait_ge(s_pair[t], 16)
                for k in range(2):
                    dve.wait_ge(s_r2, NT + 2 * t + k)
                    v.scalar_tensor_tensor(out=mine[:, t, :], in0=pair_of(t)[:, k, :], scalar=gate_w[k][:, t:t + 1],
                                           in1=mine[:, t, :], op0=ALU.mult, op1=ALU.add).then_inc(s_r2, 1)
                dve.wait_ge(s_r2, NT + 2 * t + 2)
                for half in range(2):
                    norm_stats(t, half, s_bn2)
                norm_variance(t, s_bn2, 3 * t + 2, s_ve2)

            norm_tiles(expert_sum, s_rs2, s_ln2, s_lnw2, turned_2, s_x2hi, s_x2lo)
            dve.wait_ge(s_ghi, 4)
            v.tensor_tensor(group(w_lo, OSLOT[3]), y_flat[:, GW:2 * GW].rearrange("p (u c) -> p u c", u=4),
                            group(w_hi, OSLOT[3]).bitcast(F32), ALU.subtract).then_inc(s_glo3, 1)
            for u in range(2 * NT):
                half, t = u // NT, u % NT
                dve.wait_ge(s_sig, u + 1)
                o = raw[:, t * DM + half * 512:t * DM + (half + 1) * 512]
                v.tensor_tensor(o, o, ple[:, t, half * 512:(half + 1) * 512], ALU.mult).then_inc(s_mix, 1)
                dve.wait_ge(s_mix, 2 * u + 1)
                v.tensor_tensor(o, o, mine[:, t, half * 512:(half + 1) * 512], ALU.add).then_inc(s_mix, 1)

        @block.tensor
        def _(pe):
            t_ = nc.tensor

            def three(o, lh, ll, rh, rl, first, last):
                t_.matmul(o, lh, rh, start=first, stop=False)
                t_.matmul(o, lh, rl, start=False, stop=False)
                return t_.matmul(o, ll, rh, start=False, stop=last)

            def project(n):
                grp, j = kind(n)
                i = piece_at(n)
                if n >= 2:
                    pe.wait_ge(s_evac, n - 1)
                if 2 <= n < SMALL + 2:
                    pe.wait_ge(s_ilo, n - 1)
                o = proj_bank[n % 2]
                if i is not None:
                    pe.wait_ge(s_wlo, i + 1)
                    wh, wl = (ring(m, i).rearrange("p (k c) -> p k c", k=NK) for m in (w_hi, w_lo))
                    for k in range(NK):
                        if n == 0 and k % 2 == 0:
                            pe.wait_ge(s_xlo, k // 2 + 1)
                        mm = three(o[:, :], wh[:, k, :], wl[:, k, :], a_hi[:, k, :], a_lo[:, k, :],
                                   k == 0, k == NK - 1)
                else:
                    pe.wait_ge(s_widelo, grp + 1)
                    wh, wl = (wide(m).rearrange("p (k c) -> p k c", k=NK) for m in (w_hi, w_lo))
                    t = j - TALL
                    for k in range(NK):
                        mm = three(o[:, 0:WIDE], a_hi[:, k, t * P:(t + 1) * P], a_lo[:, k, t * P:(t + 1) * P],
                                   wh[:, k, :], wl[:, k, :], k == 0, k == NK - 1)
                mm.then_inc(s_proj, 1)

            def gates_a():
                pe.wait_ge(s_w16s, 2)
                for t in range(NT):
                    for k in range(NK):
                        mm = three(lstm_bank[0][:, t * 16:(t + 1) * 16], a_hi[:, k, t * P:(t + 1) * P],
                                   a_lo[:, k, t * P:(t + 1) * P], w16_hi[:, k, :], w16_lo[:, k, :],
                                   k == 0, k == NK - 1)
                mm.then_inc(s_gate_p, 1)
                pe.wait_ge(s_setup, 16)
                pe.wait_ge(s_gate_e, 2)
                for t in range(NT):
                    t_.transpose(lstm_bank[1][0:HM, t * P:(t + 1) * P], if_pre[:, t, 0:4], ident[:, :])
                    mm = t_.transpose(turn_bank[0:HM, t * P:(t + 1) * P], if_pre[:, t, 4:8], ident[:, :])
                mm.then_inc(s_row_p, 1)

            def gates_b():
                pe.wait_ge(s_row_v, 10)
                for t in range(NT):
                    mm = t_.transpose(lstm_bank[0][:, t * HM:(t + 1) * HM], i_row[:, t * P:(t + 1) * P],
                                      ident[0:HM, 0:HM])
                mm.then_inc(s_col_p, 1)
                pe.wait_ge(s_row_a, 3)
                for t in range(NT):
                    mm = t_.transpose(lstm_bank[0][:, 16 + t * HM:16 + (t + 1) * HM], g_row[:, t * P:(t + 1) * P],
                                      ident[0:HM, 0:HM])
                mm.then_inc(s_col_p, 1)

            def index_scores():
                pe.wait_ge(s_ilo, SMALL)
                for n in range(3 * HI_):
                    b, h = n // HI_ + 1, n % HI_
                    if n == 3:
                        pe.wait_ge(s_row_v, 2)
                    if n >= 4:
                        pe.wait_ge(s_relu, n - 3)
                    rows = slice(DI * (h % 4), DI * (h % 4 + 1))
                    q, k = [[m[rows, i, c] for m in (index_hi, index_lo)]
                            for i, c in ((h // 4, slice(b * P, (b + 1) * P)), (2, slice(0, (b + 1) * P)))]
                    three(index_bank[n % 4][:, 0:(b + 1) * P], *q, *k, True, True).then_inc(s_idx, 1)

            def qk(g, u):
                U, hh, b = 8 * g + u, u // NT, u % NT
                if u == 0:
                    pe.wait_ge(s_evac, step_no(g, 1) + 1)
                if U >= 2:
                    pe.wait_ge(s_masked, U - 1)
                else:
                    pe.wait_ge(s_relu, 3 * HI_)
                rows = slice(DA * hh, DA * (hh + 1))
                t_.matmul(score_bank[U % 2][:, 0:(b + 1) * P], q_t[rows, g % 2, b * P:(b + 1) * P],
                          k_t[rows, g % 2, 0:(b + 1) * P], start=True, stop=True).then_inc(s_qk, 1)

            def turn(g, u):
                U, b = 8 * g + u, u % NT
                pe.wait_ge(s_exp, U + 1)
                if U:
                    pe.wait_ge(s_probt, U)
                for s in range(b + 1):
                    mm = t_.transpose(turn_bank[:, s * P:(s + 1) * P], prob[:, U % 2, s * P:(s + 1) * P], ident[:, :])
                mm.then_inc(s_turn, 1)

            def pv(g, u):
                U, hh, b = 8 * g + u, u // NT, u % NT
                pe.wait_ge(s_probt, U + 1)
                if u == 0:
                    pe.wait_ge(s_evac, step_no(g, STEPS - 1) + 1)
                    if g:
                        pe.wait_ge(s_ya, g)
                o = attn_bank[:, (2 * b + hh) * DA:(2 * b + hh + 1) * DA]
                for s in range(b + 1):
                    mm = t_.matmul(o, prob_t[:, U % 2, s * P:(s + 1) * P], v_a[:, g % 2, s, hh * DA:(hh + 1) * DA],
                                   start=s == 0, stop=s == b)
                mm.then_inc(s_pv, 1)

            def lstm_broadcast(h):
                if h:
                    pe.wait_ge(s_hid, 2 * h)
                else:
                    pe.wait_ge(s_col_v, 2)
                t_.matmul(lstm_bank[1][:, :], sel_head[:, h, :], nega_row, start=True, stop=True).then_inc(s_gbc, 1)

            def lstm_qk(h, b):
                if b == 0:
                    pe.wait_ge(s_conv, 2 * (h + 1))
                    if h:
                        pe.wait_ge(s_hid, 2 * h)
                elif b == 1:
                    pe.wait_ge(s_gadd, 4 * (h + 1))
                else:
                    pe.wait_ge(s_mw, 4 * h + b - 1)
                t_.matmul(lstm_bank[b % 2][:, 0:SEQ - b * P], qk_m[:, 1, b * P:(b + 1) * P], qk_m[:, 0, b * P:SEQ],
                          start=True, stop=True).then_inc(s_mqk, 1)

            def lstm_num(h):
                pe.wait_ge(s_mw, 4 * (h + 1))
                pe.wait_ge(s_evac, step_no(h, STEPS - 1) + 1)
                for t in range(NT):
                    o = lstm_bank[t // 2][:, (t % 2) * 129:(t % 2 + 1) * 129]
                    for s in range(t + 1):
                        mm = t_.matmul(o, weight[:, LO_[s] + (t - s) * P:LO_[s] + (t - s + 1) * P],
                                       v_m[:, h % 2, s, :], start=s == 0, stop=s == t)
                mm.then_inc(s_mnum, 1)

            def attention(g, j):
                for e in range(2):
                    if j < 4:
                        qk(g, 2 * j + e)
                    if 1 <= j <= 4:
                        turn(g, 2 * j - 2 + e)
                    if 2 <= j <= 5:
                        pv(g, 2 * j - 4 + e)

            def work(g, j):
                if g and j == 0:
                    lstm_num(g - 1)
                if g and j < 4:
                    attention(g - 1, j + 2)
                if g < NG:
                    if j == 3:
                        lstm_broadcast(g)
                    if j >= 6:
                        lstm_qk(g, 2 * j - 12)
                        lstm_qk(g, 2 * j - 11)
                    if j >= 6:
                        attention(g, j - 6)

            for n in range(SMALL):
                project(n)
                if n == 1:
                    gates_a()
            index_scores()
            for g in range(NG):
                for j in range(STEPS):
                    project(step_no(g, j))
                    if g == 0 and j == 0:
                        gates_b()
                    work(g, j)
            pe.wait_ge(s_evac, NSTEP)
            for j in range(NG):
                work(NG, j)
                pe.wait_ge(s_ya, j + 1)
                pe.wait_ge(s_ym, j + 1)
                for half in range(2):
                    if j:
                        pe.wait_ge(s_ylo, 2 * j + half - 1)
                    k = 4 * half + j
                    for t in range(NT):
                        mm = t_.transpose(proj_bank[half][:, t * P:(t + 1) * P], y[:, t, k * P:(k + 1) * P],
                                          ident[:, :])
                    mm.then_inc(s_yt, 1)
            pe.wait_ge(s_ylo, NK)

            def token_major(q, t, first_half):
                o = bank[first_half + t if q < 2 else 4 - first_half + t]
                wh, wl = group(w_hi, OSLOT[q]), group(w_lo, OSLOT[q])
                for kk in range(4):
                    k = 4 * (q % 2) + kk
                    mm = three(o[:, :], a_hi[:, k, t * P:(t + 1) * P], a_lo[:, k, t * P:(t + 1) * P],
                               wh[:, kk, :], wl[:, kk, :], k == 0, k == NK - 1)
                return mm

            for q in range(4):
                pe.wait_ge(s_olo, q + 1)
                for t in range(NT):
                    mm = token_major(q, t, 4)
                    if q == 3:
                        mm.then_inc(s_wot, 1)
                if q < 3:
                    mm.then_inc(s_wo, 1)

            def turn_tile(t, banks, done, low):
                for half in range(2):
                    u = 2 * t + half
                    if u >= 4:
                        pe.wait_ge(low, u - 3)
                    for k in range(4):
                        mm = t_.transpose(banks[u % 4][:, k * P:(k + 1) * P],
                                          mine[:, t, (4 * half + k) * P:(4 * half + k + 1) * P], ident[:, :])
                    mm.then_inc(done, 1)

            wr_hi = w_hi[:, WR_AT:3 * GW].rearrange("p (k c) -> p k c", k=NK)
            wr_lo = w_lo[:, WR_AT:3 * GW].rearrange("p (k c) -> p k c", k=NK)

            def route(t):
                pe.wait_ge(s_x1lo, 2 * t + 2)
                for k in range(NK):
                    mm = three(bank[4][:, t * 36:(t + 1) * 36], a_hi[:, k, t * P:(t + 1) * P],
                               a_lo[:, k, t * P:(t + 1) * P], wr_hi[:, k, :], wr_lo[:, k, :], k == 0, k == NK - 1)
                if t == NT - 1:
                    mm.then_inc(s_rp, 1)

            for t in range(NT):
                pe.wait_ge(s_ln, 2 * t + 2)
                turn_tile(t, turned_1, s_x1t, s_x1lo)
                if t == 1:
                    pe.wait_ge(s_wrs, 2)
                if t:
                    route(t - 1)
            route(NT - 1)

            def places():
                pe.wait_ge(s_cho, 1)
                pe.wait_ge(s_rc, 7)
                for t in range(NT):
                    for s in range(t + 1):
                        t_.matmul(bank[6][:, t * NE:(t + 1) * NE], tri[:, :] if s == t else ones[:, :], chosen[:, s, :],
                                  start=s == 0, stop=s == t)
                for s in range(NT):
                    mm = t_.matmul(bank[6][:, NT * NE:(NT + 1) * NE], ones[:, :], chosen[:, s, :], start=s == 0,
                                   stop=s == NT - 1)
                mm.then_inc(s_pos, 1)

            places()

            def tables(b):
                pe.wait_ge(s_tb, TB_SEATS + TB * b)
                for part, cols in enumerate((tok, (one[0], twice))):
                    for k in range(2):
                        for t in range(NT):
                            mm = t_.matmul(bank[7][:, part * NE:(part + 1) * NE], seat[k][:, t, :], cols[k][:, t, :],
                                           start=k == 0 and t == 0, stop=k == 1 and t == NT - 1)
                mm.then_inc(s_tabp, 1)

            def turn_tokens(T, par, half, first=False):
                if half == 0:
                    pe.wait_ge(s_got[par], arrived(T, par))
                if not first:
                    pe.wait_ge(s_xl, 2 * T - 1 + half)
                for k in range(4):
                    mm = t_.transpose(bank[2 + half][:, k * P:(k + 1) * P],
                                      x_got[par][:, (4 * half + k) * P:(4 * half + k + 1) * P], ident[:, :])
                mm.then_inc(s_xt, 1)

            def run(b, base):
                tables(b)
                for half in range(2):
                    turn_tokens(base, 0, half, isinstance(b, int))

                def gate_up(T, par, q):
                    pe.wait_ge(s_elo, 2 * T + q + 1)
                    for kk in range(4):
                        k = 4 * q + kk
                        mm = three(gu_bank[par][:, :], xg(hi_flat, par)[:, k, :], xg(lo_flat, par)[:, k, :],
                                   group(w_hi, ESLOT[q])[:, kk, :], group(w_lo, ESLOT[q])[:, kk, :],
                                   k == 0, k == NK - 1)
                    mm.then_inc(s_gu, 1)

                def turn_hidden(T):
                    pe.wait_ge(s_h, T + 1)
                    for k in range(2):
                        mm = t_.transpose(bank[1][:, k * P:(k + 1) * P], h_buf[:, k * P:(k + 1) * P], ident[:, :])
                    mm.then_inc(s_th, 1)

                def down(T):
                    pe.wait_ge(s_hl, T + 1)
                    pe.wait_ge(s_elo2, T + 1)
                    wait_count(pe, s_outa, T)
                    wait_count(pe, s_outv, T)
                    for half in range(2):
                        for k in range(2):
                            u = 2 * half + k
                            mm = three(bank[4 + half][:, :], ht(hi_flat)[:, k, :], ht(lo_flat)[:, k, :],
                                       group(w_hi, ESLOT[2])[:, u, :], group(w_lo, ESLOT[2])[:, u, :],
                                       k == 0, k == 1)
                    mm.then_inc(s_dn, 1)

                def step(T, par, first=False, last=False):
                    pe.wait_ge(s_xl, 2 * T + 2)
                    gate_up(T, par, 0)
                    if not first:
                        turn_hidden(T - 1)
                    gate_up(T, par, 1)
                    if not last:
                        turn_tokens(T + 1, 1 - par, 0)
                        turn_tokens(T + 1, 1 - par, 1)
                    if not first:
                        down(T - 1)

                step(base, 0, first=True)
                step(base + 1, 1)
                with pe.Fori(1, NE // 2 - 1) as i:
                    for par in range(2):
                        step(base + 2 * i + par, par)
                step(base + NE - 2, 0)
                step(base + NE - 1, 1, last=True)
                turn_hidden(base + NE - 1)
                down(base + NE - 1)

            pe.wait_ge(s_most, 1)
            expert_blocks(pe, run)

            pe.wait_ge(s_plo, 2)
            for u in range(2 * NT):
                t, half = u // 2, u % 2
                if u >= 4:
                    pe.wait_ge(s_pev, u - 3)
                for k in range(2):
                    mm = three(bank[u % 4][:, :], a_hi[:, k, t * P:(t + 1) * P], a_lo[:, k, t * P:(t + 1) * P],
                               group(w_hi, 0)[:, 2 * half + k, :], group(w_lo, 0)[:, 2 * half + k, :],
                               k == 0, k == 1)
                mm.then_inc(s_pp, 1)
            pe.wait_ge(s_pev, 2 * NT)

            def gate_half(t, half):
                pe.wait_ge(s_x2lo, 2 * t + 2)
                for q in (2 * half, 2 * half + 1):
                    pe.wait_ge(*((s_glo, q + 1) if q < 3 else (s_glo3, 1)))
                    mm = token_major(q, t, 4)
                mm.then_inc(s_gt, 1)

            for t in range(NT):
                pe.wait_ge(s_ln2, 2 * t + 2)
                turn_tile(t, turned_2, s_x2t, s_x2lo)
                if t:
                    gate_half(t - 1, 0)
            gate_half(NT - 1, 0)
            for t in range(NT):
                gate_half(t, 1)


def layout(x, p, w_in, b_igate, b_fgate, conv_w, conv_b, gn_w, w_out, ln1_g, ln1_b, router_group_w, router_group_b,
           router_expert_w, router_expert_b, expert_w_gate, expert_w_up, expert_w_down, ln2_g, ln2_b, ple_gate_w,
           ple_proj_w):
    import numpy as np

    def rows(w):
        return w.reshape(w.shape[0] // P, P, w.shape[1]).transpose(1, 0, 2)

    def halves(w, parts):
        k = w.shape[0] // P
        w = w.reshape(parts, k // parts, P, 2, 512).transpose(3, 0, 2, 1, 4)
        return w.reshape(2 * parts, P, k // parts * 512)

    def experts(gate, up, down):
        gu = np.stack([w.reshape(NE, NK, P, DE) for w in (gate, up)], axis=3).transpose(0, 2, 1, 3, 4)
        dn = down.reshape(NE, 2, P, 2, 512).transpose(0, 2, 3, 1, 4)
        return np.concatenate([gu.reshape(NE, P, 2 * GW), dn.reshape(NE, P, GW)], axis=2)

    wi = np.asarray(w_in)[0]
    at = np.cumsum([0, 512, 512, 512, 256, 32, 8, 512, 512, 512, 512, 4, 4])
    qa, ka, va, qi, ki, wx, qm, km, vm, om, im, fm = (wi[:, at[i]:at[i + 1]] for i in range(12))
    pieces = [qi[:, 0:P], qi[:, P:2 * P], np.concatenate([ki] * 4, axis=1)]
    for g in range(NG):
        pieces += [m[:, g * P:(g + 1) * P] for m in (qa, ka, qm, km)]
    wides = [np.concatenate([m[:, g * P:(g + 1) * P] for m in (va, vm, om)], axis=1) for g in range(NG)]
    cw, cb = np.asarray(conv_w)[0], np.asarray(conv_b)[0]
    return {
        "xT": rows(np.asarray(x)[0].T),
        "w_in": np.stack([rows(w).reshape(P, PW) for w in pieces]),
        "w_wide": np.stack([rows(w).reshape(P, NK * WIDE) for w in wides]),
        "w16": rows(np.concatenate([wx, im, fm], axis=1)),
        "if_bias": np.concatenate([np.asarray(b_igate)[0], np.asarray(b_fgate)[0]]),
        "conv_wb": np.concatenate([cw, cb[None]]).reshape(5, 2 * HM, P).transpose(2, 1, 0),
        "gn_w": np.asarray(gn_w)[0],
        "x": np.asarray(x)[0],
        "pT": rows(np.asarray(p)[0, 0].T),
        "w_out": halves(np.asarray(w_out)[0], 2),
        "ple_gate": halves(np.asarray(ple_gate_w)[0], 2),
        "ple_proj": halves(np.asarray(ple_proj_w)[0], 1).transpose(1, 0, 2).reshape(P, GW),
        "ln1_g": np.asarray(ln1_g)[0], "ln1_b": np.asarray(ln1_b)[0],
        "ln2_g": np.asarray(ln2_g)[0], "ln2_b": np.asarray(ln2_b)[0],
        "w_router": rows(np.concatenate([np.asarray(router_group_w)[0], np.asarray(router_expert_w)[0]], axis=1)),
        "r_bias": np.concatenate([np.asarray(router_group_b)[0], np.asarray(router_expert_b)[0]]),
        "w_exp": experts(*(np.asarray(w)[0] for w in (expert_w_gate, expert_w_up, expert_w_down))),
    }


def kernel(**inputs):
    import numpy as _np
    import concourse.bacc as _bacc
    from concourse import mybir as _mybir
    from concourse.bass_utils import run_bass_kernel_spmd as _run

    nc = _bacc.Bacc("TRN2", target_bir_lowering=False, num_devices=1)
    arrays, views = {}, {}
    for name, a in layout(**inputs).items():
        a = _np.ascontiguousarray(a)
        arrays[f"in_{name}_dram"] = a
        views[name] = nc.dram_tensor(f"in_{name}_dram", a.shape, _mybir.dt.from_np(a.dtype), kind="ExternalInput").ap()
    out = nc.dram_tensor("out_dram", (SEQ, DM), _mybir.dt.float32, kind="ExternalOutput").ap()
    x1 = nc.dram_tensor("x1_dram", (SEQ, DM), _mybir.dt.float32, kind="Internal").ap()
    pairs = nc.dram_tensor("pair_dram", (2 * SEQ, DM), _mybir.dt.float32, kind="Internal").ap()
    hybrid_layer(nc, views, out, x1, pairs)
    r = _run(nc, [arrays], core_ids=[0])
    return r.results[0]["out_dram"].reshape(1, SEQ, DM)
```
